# Optimizing a Trainium2 kernel written in Bass

```python
import math
import jax, jax.numpy as jnp
from jax import lax
import numpy as np

D_MODEL = 1024
BATCH = 1
SEQ = 128
DEPTH = 2
DEC_BATCH = 1
DEC_SEQ = 256
PAST_LEN = 128

GRID_W = 64
ROPE_BASE = 10000.0
NORM_EPS = 1e-6
N_MIXERS = 2
N_ATTN_LAYERS = (DEPTH + 1) // 2
N_RET_LAYERS = DEPTH // 2
DA_HEADS = 8
DA_HEAD_DIM = 64
DA_V_DIM = 2 * DA_HEAD_DIM
DA_QK_WIDTH = DA_HEADS * 2 * DA_HEAD_DIM
DA_QBLOCK = 128
RET_HEADS = 4
RET_DK = D_MODEL // RET_HEADS
RET_DV = 2 * RET_DK
RET_CHUNK = 128
N_EXPERTS = 16
N_GROUPS = 4
EXPERTS_PER_GROUP = N_EXPERTS // N_GROUPS
TOP_K = 2
D_EXPERT = D_MODEL // 2

kernel_name = 'hybrid_diffattn_retention_groupmoe_denoise_step'

F32 = jnp.float32

def rmsnorm(x, g):
    xf = x.astype(F32)
    y = xf * lax.rsqrt(jnp.mean(xf * xf, axis=-1, keepdims=True) + NORM_EPS) * g.astype(F32)
    return y.astype(x.dtype)

def head_groupnorm(o):
    mu = jnp.mean(o, axis=-1, keepdims=True)
    var = jnp.mean(jnp.square(o - mu), axis=-1, keepdims=True)
    return (o - mu) * lax.rsqrt(var + NORM_EPS)

def ada_modulation(cond, w, b):
    m = jax.nn.silu(cond) @ w + b
    return [t[:, None, :] for t in jnp.split(m, 6, axis=-1)]

def axial_rope(x):
    n, d = x.shape[1], x.shape[-1]
    n_rows = n // GRID_W
    row = jnp.repeat(jnp.arange(n_rows), GRID_W).astype(F32)
    col = jnp.tile(jnp.arange(GRID_W), n_rows).astype(F32)
    nf = d // 4
    freqs = jnp.power(ROPE_BASE, -jnp.arange(nf, dtype=F32) / nf)
    ang = jnp.concatenate([row[:, None] * freqs, col[:, None] * freqs], axis=-1)
    shape = (n,) + (1,) * (x.ndim - 3) + (d // 2,)
    cos = jnp.cos(ang).reshape(shape)
    sin = jnp.sin(ang).reshape(shape)
    xf = x.astype(F32)
    x1, x2 = xf[..., : d // 2], xf[..., d // 2:]
    return jnp.concatenate([x1 * cos - x2 * sin, x2 * cos + x1 * sin], axis=-1).astype(x.dtype)

def diff_attn_blocks(q, k, v, lam):
    B, N = q.shape[:2]
    nb = N // DA_QBLOCK
    qb = q.reshape(B, nb, DA_QBLOCK, DA_HEADS, 2, DA_HEAD_DIM).swapaxes(0, 1)
    scale = DA_HEAD_DIM ** -0.5

    def block(qi):
        s = jnp.einsum('bqhcd,bkhcd->bchqk', qi, k, preferred_element_type=F32) * scale
        p = jax.nn.softmax(s, axis=-1)
        a = p[:, 0] - lam * p[:, 1]
        return jnp.einsum('bhqk,bkhe->bqhe', a.astype(v.dtype), v)

    o = lax.map(block, qb)
    return o.swapaxes(0, 1).reshape(B, N, DA_HEADS, DA_V_DIM)

def diff_attention(h, w_qkv, lq1, lk1, lq2, lk2, subln_g, w_o, lam_init, cached):
    B, N, _ = h.shape
    qkv = h @ w_qkv
    q = qkv[..., :DA_QK_WIDTH].reshape(B, N, DA_HEADS, 2, DA_HEAD_DIM)
    k = qkv[..., DA_QK_WIDTH:2 * DA_QK_WIDTH].reshape(B, N, DA_HEADS, 2, DA_HEAD_DIM)
    v = qkv[..., 2 * DA_QK_WIDTH:].reshape(B, N, DA_HEADS, DA_V_DIM)
    if cached is None:
        keys, vals = k, v
    else:
        q = axial_rope(q)
        keys = jnp.concatenate([cached[0], axial_rope(k)], axis=1)
        vals = jnp.concatenate([cached[1], v], axis=1)
    lam = (jnp.exp(jnp.sum(lq1.astype(F32) * lk1.astype(F32)))
           - jnp.exp(jnp.sum(lq2.astype(F32) * lk2.astype(F32))) + lam_init)
    o = diff_attn_blocks(q, keys, vals, lam)
    o = rmsnorm(o, subln_g) * (1.0 - lam_init)
    return o.reshape(B, N, DA_HEADS * DA_V_DIM) @ w_o, (k, v)

def retention_scan(q, k, v, log_g, s0):
    B, N, H, _ = q.shape
    C = RET_CHUNK
    nc = N // C

    def chunks(t):
        return t.astype(F32).reshape(B, nc, C, H, t.shape[-1]).swapaxes(0, 1)

    qc, kc, vc = chunks(q), chunks(k), chunks(v)
    idx = jnp.arange(C, dtype=F32)
    rel = idx[:, None] - idx[None, :]
    intra = jnp.exp(jnp.where(rel[None] >= 0, rel[None] * log_g[:, None, None], -jnp.inf))
    q_decay = jnp.exp((idx[:, None] + 1.0) * log_g[None, :])[None, :, :, None]
    k_decay = jnp.exp((C - 1.0 - idx)[:, None] * log_g[None, :])[None, :, :, None]
    chunk_decay = jnp.exp(C * log_g)[None, :, None, None]

    def step(s, inp):
        qi, ki, vi = inp
        a = jnp.einsum('bihd,bjhd->bhij', qi, ki) * intra
        o = (jnp.einsum('bhij,bjhe->bihe', a, vi)
             + jnp.einsum('bihd,bhde->bihe', qi, s) * q_decay)
        s = chunk_decay * s + jnp.einsum('bjhd,bjhe->bhde', ki * k_decay, vi)
        return s, o

    s, o = lax.scan(step, s0.astype(F32), (qc, kc, vc))
    return o.swapaxes(0, 1).reshape(B, N, H, v.shape[-1]), s

def retention(h, w_qkv, w_g_f, w_g_b, decay_f, decay_b, w_o, cached):
    B, N, _ = h.shape
    kd = RET_HEADS * RET_DK
    qkv = h @ w_qkv
    q = qkv[..., :kd].reshape(B, N, RET_HEADS, RET_DK)
    k = qkv[..., kd:2 * kd].reshape(B, N, RET_HEADS, RET_DK) * (RET_DK ** -0.5)
    v = qkv[..., 2 * kd:].reshape(B, N, RET_HEADS, RET_DV)
    if cached is None:
        s0f = jnp.zeros((B, RET_HEADS, RET_DK, RET_DV), F32)
        s0b = s0f
    else:
        q, k = axial_rope(q), axial_rope(k)
        s0f, s0b = cached
    lg_f = jax.nn.log_sigmoid(decay_f.astype(F32))
    lg_b = jax.nn.log_sigmoid(decay_b.astype(F32))
    o_f, s_f = retention_scan(q, k, v, lg_f, s0f)
    o_b, s_b = retention_scan(q[:, ::-1], k[:, ::-1], v[:, ::-1], lg_b, s0b)
    o_b = o_b[:, ::-1]
    g_f = jax.nn.silu(h @ w_g_f).reshape(B, N, RET_HEADS, RET_DV).astype(F32)
    g_b = jax.nn.silu(h @ w_g_b).reshape(B, N, RET_HEADS, RET_DV).astype(F32)
    o = (head_groupnorm(o_f) * g_f + head_groupnorm(o_b) * g_b).astype(h.dtype)
    return o.reshape(B, N, RET_HEADS * RET_DV) @ w_o, (s_f.astype(h.dtype), s_b.astype(h.dtype))

def group_moe(h, w_router, router_bias, w_gate, w_up, w_down):
    B, N, D = h.shape
    t = h.reshape(B * N, D)
    s = jax.nn.sigmoid((t @ w_router).astype(F32))
    sel = s + router_bias.astype(F32)
    grp_score = lax.top_k(sel.reshape(-1, N_GROUPS, EXPERTS_PER_GROUP), 2)[0].sum(-1)
    best = jnp.argmax(grp_score, axis=-1)
    in_group = (jnp.arange(N_EXPERTS) // EXPERTS_PER_GROUP)[None, :] == best[:, None]
    _, idx = lax.top_k(jnp.where(in_group, sel, -jnp.inf), TOP_K)
    w = jnp.take_along_axis(s, idx, axis=-1)
    w = w / jnp.sum(w, axis=-1, keepdims=True)
    gates = jnp.sum(jax.nn.one_hot(idx, N_EXPERTS, dtype=F32) * w[..., None], axis=1)

    def expert(y, p):
        wg, wu, wd, ge = p
        a = jax.nn.silu(t @ wg) * (t @ wu) * ge[:, None].astype(t.dtype)
        return y + a @ wd, None

    y, _ = lax.scan(expert, jnp.zeros_like(t), (w_gate, w_up, w_down, gates.T))
    return y.reshape(B, N, D)

def trunk(x, cond, ctx_k, ctx_v, ctx_sf, ctx_sb, w_ada, b_ada, norm_mix_g, norm_ffn_g,
          final_norm_g, da_w_qkv, da_lambda_q1, da_lambda_k1, da_lambda_q2, da_lambda_k2,
          da_subln_g, da_w_o, ret_w_qkv, ret_w_gate_fwd, ret_w_gate_bwd, ret_decay_fwd,
          ret_decay_bwd, ret_w_o, w_router, router_bias, moe_w_gate, moe_w_up, moe_w_down):
    is_ctx = ctx_k is None
    new_k, new_v, new_sf, new_sb = [], [], [], []
    for i in range(DEPTH):
        sh1, sc1, g1, sh2, sc2, g2 = ada_modulation(cond, w_ada[i], b_ada[i])
        h = rmsnorm(x, norm_mix_g[i]) * (1 + sc1) + sh1
        j = i // N_MIXERS
        if i % N_MIXERS == 0:
            lam_init = 0.8 - 0.6 * math.exp(-0.3 * i)
            cached = None if is_ctx else (ctx_k[:, j], ctx_v[:, j])
            mix, (k, v) = diff_attention(h, da_w_qkv[j], da_lambda_q1[j], da_lambda_k1[j],
                                         da_lambda_q2[j], da_lambda_k2[j], da_subln_g[j],
                                         da_w_o[j], lam_init, cached)
            if is_ctx:
                new_k.append(k)
                new_v.append(v)
        else:
            cached = None if is_ctx else (ctx_sf[:, j], ctx_sb[:, j])
            mix, (sf, sb) = retention(h, ret_w_qkv[j], ret_w_gate_fwd[j], ret_w_gate_bwd[j],
                                      ret_decay_fwd[j], ret_decay_bwd[j], ret_w_o[j], cached)
            if is_ctx:
                new_sf.append(sf)
                new_sb.append(sb)
        x = x + g1 * mix
        h = rmsnorm(x, norm_ffn_g[i]) * (1 + sc2) + sh2
        x = x + g2 * group_moe(h, w_router, router_bias, moe_w_gate[i], moe_w_up[i], moe_w_down[i])
    return rmsnorm(x, final_norm_g), new_k, new_v, new_sf, new_sb

def setup_inputs(seed: int = 0) -> dict:
    key = jax.random.key(seed)
    ks = iter(jax.random.split(key, 40))

    def nrm(shape, scale):
        return jax.random.normal(next(ks), shape, F32) * scale

    D = D_MODEL
    dsd = D ** -0.5
    base_decay = jnp.log(2.0 ** (5.0 + jnp.arange(RET_HEADS, dtype=F32)) - 1.0)
    return {
        'x_prompt': nrm((BATCH, SEQ, D), 1.0),
        'x_sample': nrm((DEC_BATCH, DEC_SEQ, D), 1.0),
        'cache_attn_k': nrm((DEC_BATCH, N_ATTN_LAYERS, PAST_LEN, DA_HEADS, 2, DA_HEAD_DIM), 1.0),
        'cache_attn_v': nrm((DEC_BATCH, N_ATTN_LAYERS, PAST_LEN, DA_HEADS, DA_V_DIM), 1.0),
        'state_ret_fwd': nrm((DEC_BATCH, N_RET_LAYERS, RET_HEADS, RET_DK, RET_DV), 0.3),
        'state_ret_bwd': nrm((DEC_BATCH, N_RET_LAYERS, RET_HEADS, RET_DK, RET_DV), 0.3),
        'c': nrm((DEC_BATCH, D), 1.0),
        'c_ctx': nrm((D,), 1.0),
        'w_ada': nrm((DEPTH, D, 6 * D), 0.5 * dsd),
        'b_ada': nrm((DEPTH, 6 * D), 0.02),
        'norm_mix_g': 1.0 + nrm((DEPTH, D), 0.05),
        'norm_ffn_g': 1.0 + nrm((DEPTH, D), 0.05),
        'final_norm_g': 1.0 + nrm((D,), 0.05),
        'da_w_qkv': nrm((N_ATTN_LAYERS, D, 2 * DA_QK_WIDTH + DA_HEADS * DA_V_DIM), dsd),
        'da_lambda_q1': nrm((N_ATTN_LAYERS, DA_HEAD_DIM), 0.1),
        'da_lambda_k1': nrm((N_ATTN_LAYERS, DA_HEAD_DIM), 0.1),
        'da_lambda_q2': nrm((N_ATTN_LAYERS, DA_HEAD_DIM), 0.1),
        'da_lambda_k2': nrm((N_ATTN_LAYERS, DA_HEAD_DIM), 0.1),
        'da_subln_g': 1.0 + nrm((N_ATTN_LAYERS, DA_V_DIM), 0.05),
        'da_w_o': nrm((N_ATTN_LAYERS, DA_HEADS * DA_V_DIM, D), (DA_HEADS * DA_V_DIM) ** -0.5),
        'ret_w_qkv': nrm((N_RET_LAYERS, D, 2 * RET_HEADS * RET_DK + RET_HEADS * RET_DV), dsd),
        'ret_w_gate_fwd': nrm((N_RET_LAYERS, D, RET_HEADS * RET_DV), dsd),
        'ret_w_gate_bwd': nrm((N_RET_LAYERS, D, RET_HEADS * RET_DV), dsd),
        'ret_decay_fwd': base_decay[None, :] + nrm((N_RET_LAYERS, RET_HEADS), 0.01),
        'ret_decay_bwd': base_decay[None, :] + nrm((N_RET_LAYERS, RET_HEADS), 0.01),
        'ret_w_o': nrm((N_RET_LAYERS, RET_HEADS * RET_DV, D), (RET_HEADS * RET_DV) ** -0.5),
        'w_router': nrm((D, N_EXPERTS), dsd),
        'router_bias': nrm((N_EXPERTS,), 0.01),
        'moe_w_gate': nrm((DEPTH, N_EXPERTS, D, D_EXPERT), dsd),
        'moe_w_up': nrm((DEPTH, N_EXPERTS, D, D_EXPERT), dsd),
        'moe_w_down': nrm((DEPTH, N_EXPERTS, D_EXPERT, D), D_EXPERT ** -0.5),
    }

def reference(x_prompt, x_sample, cache_attn_k, cache_attn_v, state_ret_fwd, state_ret_bwd,
              c, c_ctx, w_ada, b_ada, norm_mix_g, norm_ffn_g, final_norm_g, da_w_qkv,
              da_lambda_q1, da_lambda_k1, da_lambda_q2, da_lambda_k2, da_subln_g, da_w_o,
              ret_w_qkv, ret_w_gate_fwd, ret_w_gate_bwd, ret_decay_fwd, ret_decay_bwd, ret_w_o,
              w_router, router_bias, moe_w_gate, moe_w_up, moe_w_down):
    weights = (w_ada, b_ada, norm_mix_g, norm_ffn_g, final_norm_g, da_w_qkv, da_lambda_q1,
               da_lambda_k1, da_lambda_q2, da_lambda_k2, da_subln_g, da_w_o, ret_w_qkv,
               ret_w_gate_fwd, ret_w_gate_bwd, ret_decay_fwd, ret_decay_bwd, ret_w_o,
               w_router, router_bias, moe_w_gate, moe_w_up, moe_w_down)
    y_prompt, ks, vs, sfs, sbs = trunk(x_prompt, c_ctx[None, :], None, None, None, None, *weights)
    y_sample, _, _, _, _ = trunk(x_sample, c, cache_attn_k, cache_attn_v, state_ret_fwd,
                                 state_ret_bwd, *weights)
    new_attn_k = jnp.stack(ks, axis=1)
    new_attn_v = jnp.stack(vs, axis=1)
    new_ret_fwd = jnp.stack(sfs, axis=1)
    new_ret_bwd = jnp.stack(sbs, axis=1)
    return (y_prompt, y_sample, new_attn_k, new_attn_v, new_ret_fwd, new_ret_bwd)


_drawn_inputs = setup_inputs


def setup_inputs(seed=0):
    import zlib

    import numpy as np

    out = dict(_drawn_inputs(seed))
    spreads = {}
    factors = {}
    for name, (base, spread) in spreads.items():
        noise = np.random.default_rng([zlib.crc32(name.encode()), seed]).standard_normal(out[name].shape)
        drawn = base * np.exp(spread * noise) if base else spread * noise
        out[name] = __import__('jax').numpy.asarray(drawn.astype(out[name].dtype))
    for name, factor in factors.items():
        out[name] = (out[name] * factor).astype(out[name].dtype)
    return out
```

```python
import math
from contextlib import ExitStack

import numpy as np

import concourse.bass as bass
from concourse import mybir

P = 128
D = 1024
KT = D // P
NP_TOK, NS_TOK = 128, 256
TOK = NP_TOK + NS_TOK
TT = TOK // P
SEG = ((0, 0, NP_TOK), (1, NP_TOK, TOK))
DEPTH = 2
EPS = 1e-6
HEADS, HD, HV = 8, 64, 128
HALF = HEADS // 2
RH, RDK, RDV = 4, 256, 512
NE, NG, EPG = 16, 4, 4
BLK = 64
MAXOV = 2 * TOK // BLK
NSLOT, SLOT = 6, 4096
NB = 8
LAM_INIT = 0.8 - 0.6 * math.exp(-0.3 * 0)
BIG = 1e30


def shape_constants():
    def angles(width):
        nf = width // 4
        row = np.repeat(np.arange(NS_TOK // 64), 64).astype(np.float32)
        col = np.tile(np.arange(64), NS_TOK // 64).astype(np.float32)
        freqs = np.power(np.float32(10000.0), -np.arange(nf, dtype=np.float32) / np.float32(nf)).astype(np.float32)
        return np.concatenate([row[:, None] * freqs, col[:, None] * freqs], axis=-1).astype(np.float32).T

    part = np.arange(P)
    base = {
        "ident": np.eye(P, dtype=np.float32),
        "before": (part[:, None] < part[None, :]).astype(np.float32),
        "iota": np.broadcast_to(np.arange(TOK, dtype=np.float32), (P, TOK)),
        "first4": np.broadcast_to(np.arange(EPG, 0, -1, dtype=np.float32), (P, NG)),
        "first16": np.broadcast_to(np.arange(NE, 0, -1, dtype=np.float32), (P, NE)),
        "row0": np.broadcast_to(np.arange(NE, dtype=np.float32) * BLK, (P, NE)),
    }
    a = angles(HD)[part % 32]
    sign = np.where(part % 64 < 32, -1.0, 1.0).astype(np.float32)[:, None]
    att = {
        "swap": (part[:, None] == (part[None, :] ^ 32)).astype(np.float32),
        "cos": np.cos(a).astype(np.float32),
        "sin": (np.sin(a) * sign).astype(np.float32),
    }
    b = angles(RDK)
    ret = {"cos": np.cos(b).astype(np.float32), "sin": np.sin(b).astype(np.float32)}
    j, u = part[:, None].astype(np.float32), np.arange(NS_TOK, dtype=np.float32)[None, :]
    dist = {
        "rel_f": np.concatenate([np.maximum(u - j, 0), P - 1 - j], 1),
        "keep_f": np.concatenate([(u >= j) * 1.0, np.ones((P, 1))], 1),
        "rel_b": np.concatenate([np.maximum(P + j - u, 0), j], 1),
        "keep_b": np.concatenate([(u <= P + j) * 1.0, np.ones((P, 1))], 1),
        "q_f": np.broadcast_to(u + 1, (P, NS_TOK)),
        "q_b": np.broadcast_to(NS_TOK - u, (P, NS_TOK)),
    }
    return base, att, ret, dist


def pack(tables):
    at, places = 0, {}
    for name, t in tables.items():
        places[name] = (at, at + t.shape[1])
        at += t.shape[1]
    return np.ascontiguousarray(np.concatenate([np.asarray(t, np.float32) for t in tables.values()], 1)), places


def plan_jobs():
    jobs = [(("small", 0), "dve"), (("small", 1), "dve")]
    jobs += [(("x", kt), "dve") for kt in range(KT)]

    def ada(layer, units):
        out = []
        for n, u in enumerate(units):
            out.append((("ada", layer, u), "act"))
            if n:
                out.append((("adaT", layer, units[n - 1]), "dve"))
        return out + [(("adaT", layer, units[-1]), "dve")]

    def moe(layer):
        out = [(("norm", 2 * layer + 1), "act"), (("logit", layer), "dve"), (("logitT", layer), "act")]
        out += [(("htok", layer, i), "act" if i % 2 else "dve") for i in range(2 * TT)]
        out += [(("rank", layer), "dve")]
        return out + [(("y", layer, ft), "dve") for ft in range(KT)]

    jobs += ada(0, range(4)) + [(("norm", 0), "act")]
    jobs += [(("ck", i), "act") for i in range(2)]
    for g in range(2):
        for kind in "qk":
            for i in range(HALF):
                h = HALF * g + i
                jobs.append(((kind, h), "act"))
                if i:
                    jobs.append(((kind + "swap", h - 1), "dve"))
            jobs.append(((kind + "swap", HALF * g + HALF - 1), "dve"))
        jobs.append((("knew", g), "act"))
        jobs += [(("v", g, t), "act") for t in range(TT)]
        for i in range(HALF + 2):
            h = HALF * g + i
            if i < HALF:
                jobs += [(("S", h, r, c), "act") for r in range(TT) for c in range(2)]
            if 1 <= i <= HALF:
                jobs += [(("aT", h - 1, r), "act") for r in range(TT)] + [(("o", h - 1), "dve")]
            if i >= 2:
                jobs.append((("oss", h - 2), "dve"))
    jobs += ada(0, range(4, 12)) + ada(1, range(12))
    jobs += [(("wo", ft), "dve") for ft in range(KT)]
    jobs += moe(0)
    jobs.append((("norm", 2), "act"))
    for h in range(RH):
        jobs += [(("rq", h, t), "act") for t in range(2)] + [(("rk", h, t), "act") for t in range(2)]
        jobs += [(("rv", h, t), "dve") for t in range(TT)]
        jobs += [(("rg", h, d, t), "act") for d in range(2) for t in range(TT)]
        if h:
            jobs += [(("roT", h - 1, t), "act") for t in range(TT)]
        jobs += [(("rkT", h), "dve"), (("rA", h, 0), "dve"), (("rA", h, 1), "dve")]
        jobs += [(("rs", h, d, t), "act") for d in range(2) for t in range(2)]
        jobs += [(("ro", h, t, d), "act") for t in range(TT) for d in range(2)]
    jobs += [(("roT", RH - 1, t), "act") for t in range(TT)]
    jobs += [(("rwo", ft), "dve") for ft in range(KT)]
    jobs += moe(1)
    jobs.append((("norm", 4), "act"))
    jobs += [(("yout", i), "act" if i % 2 else "dve") for i in range(2 * TT)]
    return jobs


def plan_units():
    units = [(("ada", 0, u), ("ada", 0, u)) for u in range(4)]
    for g in range(2):
        units += [(("q", g), ("q", HALF * g + HALF - 1)), (("k", g), ("k", HALF * g + HALF - 1)),
                  (("v", g), ("v", g, TT - 1))]
    units += [(("ada", 0, u), ("ada", 0, u)) for u in range(4, 12)] + [(("ada", 1, u), ("ada", 1, u)) for u in range(12)]
    units += [(("wo", n), ("wo", 4 * n + 3)) for n in range(2)]
    units += [(("moe", 0, n), None) for n in range(3 * NE)]
    for h in range(RH):
        units += [(("rqk", h), ("rk", h, 1)), (("rv", h), ("rv", h, TT - 1)), (("rg", h, 0), ("rg", h, 0, TT - 1)),
                  (("rg", h, 1), ("rg", h, 1, TT - 1)), (("state", h), ("ro", h, TT - 1, 1))]
    units += [(("rwo", n), ("rwo", 2 * n + 1)) for n in range(4)]
    units += [(("moe", 1, n), None) for n in range(3 * NE)]
    return units


def trunk_kernel(nc, ins, outs, scratch):
    F, I32, BF = mybir.dt.float32, mybir.dt.int32, mybir.dt.bfloat16
    ALU, ACT, AX = mybir.AluOpType, mybir.ActivationFunctionType, mybir.AxisListType
    ds = bass.ds
    y_prompt, y_sample, new_k, new_v, new_sf, new_sb = outs

    base, att, ret, dist = shape_constants()
    base_np, base_at = pack(base)
    att_np, att_at = pack(att)
    ret_np, ret_at = pack(ret)
    dist_np, dist_at = pack(dist)
    base_d = nc.inline_tensor(base_np, name="base_tables").ap()
    att_d = nc.inline_tensor(att_np, name="attention_tables").ap()
    ret_d = nc.inline_tensor(ret_np, name="retention_tables").ap()
    dist_d = nc.inline_tensor(dist_np.astype(mybir.dt.np(BF)), name="distance_tables").ap()

    JOBS = plan_jobs()
    UNITS = plan_units()
    job_no, evac_no, counts = {}, {}, {"act": 0, "dve": 0}
    for n, (name, who) in enumerate(JOBS):
        counts[who] += 1
        job_no[name] = n
        evac_no[name] = (who, counts[who])
    unit_no = {name: n for n, (name, _) in enumerate(UNITS)}
    full_at = []
    for n, (name, _) in enumerate(UNITS):
        full_at.append((full_at[n - NSLOT] if n >= NSLOT else 0) + 16 * (2 if name[0] in ("rqk", "state") else 1))
    ada_at = {(l, u): (12 * l + u) % 2 for l in range(DEPTH) for u in range(12)}

    ctx = ExitStack()
    with ctx:
        def sb(name, shape, dt=F):
            return ctx.enter_context(nc.sbuf_tensor(name, shape, dt))

        def sem(name):
            return ctx.enter_context(nc.semaphore(name))

        ring = sb("ring", [P, NSLOT, SLOT])
        xT = sb("xT", [P, KT, TOK])
        hT = sb("hT", [P, KT, TOK])
        sq = sb("sq", [P, KT, TOK])
        base_sb = sb("base_sb", [P, base_np.shape[1]])
        ones = sb("ones", [P, P])
        eps = sb("eps", [P, 1])
        cols0 = sb("cols0", [P, P])
        cols1 = sb("cols1", [P, 25])
        cond = sb("cond", [P, KT, 32])
        ada_rows = sb("ada_rows", [P, 2, 512])
        mod = sb("mod", [P, DEPTH, 48, 2])
        gain = sb("gain", [P, DEPTH, 2, KT, 2])
        rms = sb("rms", [P, TOK])
        rinv = sb("rinv", [P, TOK])
        lam_s = sb("lam_s", [P, 4])
        subg = sb("subg", [P, 1])
        dec = sb("dec", [P, 6, 2 * RH])
        rbias = sb("rbias", [P, NE])
        wr = sb("wr", [P, KT, NE])
        RT = [sb(f"route_tab{l}", [1, NE + 1], I32) for l in range(DEPTH)]
        sq_row = sq[:, :, :].rearrange("p k t -> p (k t)")
        rows0, rows1 = sq_row[:, 0:P], sq_row[0:25, P:2 * P]
        lamrow = sq_row[:, 2 * P:2 * P + 4 * HD].rearrange("p (n d) -> p n d", n=4)
        lam_p = sq_row[:, 4 * P:4 * P + 2 * HD].rearrange("p (n d) -> p n d", n=2)
        zrow = hT[:, :, :].rearrange("p k t -> p (k t)")[:, 0:D]
        WCOLS = (nc.sbuf_bytes_remaining - 64) // 4
        work = sb("work", [P, WCOLS])

        def carve(sizes):
            at, out = 0, {}
            for name, n in sizes.items():
                assert at + n <= WCOLS, (name, at + n, WCOLS)
                out[name] = work[:, at:at + n]
                at += n
            return out

        def table(tile, at, name):
            return tile[:, at[name][0]:at[name][1]]

        ident = table(base_sb, base_at, "ident")
        before = table(base_sb, base_at, "before")
        iota = table(base_sb, base_at, "iota")

        wa = carve({"tab": att_np.shape[1], "qz": 2 * HALF * TOK, "kT": HALF * TOK, "v": TT * 512, "ck": KT * P,
                    "cv": D, "raw": 2 * TOK, "t1": 2 * NS_TOK, "t2": NS_TOK, "pr": 4 * TOK, "a": TT * TOK,
                    "aTp": P, "aTs": 3 * NS_TOK, "ss": HALF * TOK, "nm": 12, "sm": 12, "rc": 6})
        xtok = wa["qz"].rearrange("p (t d) -> p t d", t=TT)
        att_tab = wa["tab"]
        qz = wa["qz"].rearrange("p (c h t) -> p c h t", c=2, h=HALF)
        kT = wa["kT"].rearrange("p (h t) -> p h t", h=HALF)
        vtok = wa["v"].rearrange("p (t d) -> p t d", t=TT)
        ckT = wa["ck"].rearrange("p (h t) -> p h t", h=KT)
        cvt = wa["cv"]
        cktok = wa["pr"][:, 0:D]
        raw = wa["raw"].rearrange("p (n t) -> p n t", n=2)
        t1 = wa["t1"].rearrange("p (n t) -> p n t", n=2)
        t2 = wa["t2"]
        pr = wa["pr"].rearrange("p (n c t) -> p n c t", n=2, c=2)
        aw = wa["a"].rearrange("p (n t) -> p n t", n=TT)
        aTp = wa["aTp"]
        aTs = wa["aTs"].rearrange("p (k t) -> p k t", k=3)
        osq = ada_rows[:, :, 0:TOK]
        ss = wa["ss"].rearrange("p (h t) -> p h t", h=HALF)
        nm = wa["nm"].rearrange("p (n c) -> p n c", c=2)
        sm = wa["sm"].rearrange("p (n c) -> p n c", c=2)
        rc = wa["rc"]
        ko = wa["ss"][:, 0:512]
        oT = sq

        wr_ = carve({"tab": ret_np.shape[1], "dist": (dist_np.shape[1] + 1) // 2, "q": 2 * TOK, "k": 2 * TOK,
                     "tmp": 2 * 2 * NS_TOK, "v": TT * RDV, "g": 2 * TT * RDV, "E": 2 * 258, "qe": 2 * NS_TOK,
                     "qd": 2 * 2 * NS_TOK, "A": 2 * 512, "n": 2 * RDV, "o": TT * RDV, "kd": 2 * RDK,
                     "st": RDV, "bst": 12, "mv": 4, "nw": 14})
        ret_tab = wr_["tab"]
        dist_tab = wr_["dist"].bitcast(BF)
        rq = wr_["q"].rearrange("p (n t) -> p n t", n=2)
        rk = wr_["k"].rearrange("p (n t) -> p n t", n=2)
        rtmp = wr_["tmp"].rearrange("p (m n t) -> p m n t", m=2, n=2)
        rv = wr_["v"].rearrange("p (t d) -> p t d", t=TT)
        rg = wr_["g"].rearrange("p (e t d) -> p e t d", e=2, t=TT)
        rE = wr_["E"].rearrange("p (e u) -> p e u", e=2)
        qe = wr_["qe"].rearrange("p (e u) -> p e u", e=2)
        qd = wr_["qd"].rearrange("p (e n t) -> p e n t", e=2, n=2)
        rA = wr_["A"].rearrange("p (e u) -> p e u", e=2)
        rn = wr_["n"].rearrange("p (e u) -> p e u", e=2)
        ro = wr_["o"].rearrange("p (n u) -> p n u", n=TT)
        kd = wr_["kd"].rearrange("p (e u) -> p e u", e=2)
        st = wr_["st"]
        bst = wr_["bst"].rearrange("p (n s) -> p n s", n=2)
        mv = wr_["mv"].rearrange("p (n s) -> p n s", n=2)
        nw = wr_["nw"]

        def roT(f):
            return sq[:, f, :] if f < KT else hT[:, f - KT, :]

        wm = carve({"htok": TT * D, "xs": 2 * D, "sel": TT * P, "sg": 2 * 512, "a": 2 * 512, "aT": 2 * 256,
                    "y": 2 * 512, "osel": TT * BLK, "ox": 512, "osg": 512, "oa": 512, "oaT": 256, "oy": 512,
                    "yg": TT * D, "lg": TOK, "s": TT * NE, "selb": TT * NE, "pair": TT * NG * 6, "gs": TT * NG,
                    "gm": TT, "gw": TT * NG, "gx": TT, "ing": TT * NG, "pen": TT * NG, "mx": TT, "w": TT * NE,
                    "wx": TT, "m": 2 * TT * NE, "pick": TT * NE, "wt": 2 * TT, "M": TT * NE, "rk": (TT + 1) * NE,
                    "nov": NE, "cum": NE + 1, "R": TT * (NE + 2), "hi": TT * NE, "dd": NE, "row": 2 * TT,
                    "idx": 2 * TT, "den": TT})
        htok = wm["htok"].rearrange("p (t d) -> p t d", t=TT)
        xs = wm["xs"].rearrange("p (n k s) -> p n k s", n=2, k=KT)
        sel = wm["sel"].rearrange("p (t x s) -> p t x s", t=TT, x=2)
        sg = wm["sg"].rearrange("p (x f) -> p x f", x=2)
        ea = wm["a"].rearrange("p (x f) -> p x f", x=2)
        eaT = wm["aT"].rearrange("p (x k s) -> p x k s", x=2, k=4)
        ysb = wm["y"].rearrange("p (x f) -> p x f", x=2)
        osel = wm["osel"].rearrange("p (t s) -> p t s", t=TT)
        ox = wm["ox"].rearrange("p (k s) -> p k s", k=KT)
        osg, oa, oy = wm["osg"], wm["oa"], wm["oy"]
        oaT = wm["oaT"].rearrange("p (k s) -> p k s", k=4)
        yg = [wm["yg"].rearrange("p (t d) -> p t d", t=TT), hT[:, :, :].rearrange("p k t -> p (k t)").rearrange("p (t d) -> p t d", t=TT)]
        ytok = sq[:, :, :].rearrange("p k t -> p (k t)").rearrange("p (t d) -> p t d", t=TT)

        def yo(i):
            return wm["htok"][:, 512 * i:512 * i + 512]

        def v3(name, *dims):
            ap = wm[name]
            if len(dims) == 1:
                return ap.rearrange("p (a b) -> p a b", a=dims[0])
            return ap.rearrange("p (a b c) -> p a b c", a=dims[0], b=dims[1])

        psum = ctx.enter_context(nc.psum_tensor("psum", [P, NB, 512], F))

        ps_filled = sem("ps_filled")
        evac = {"act": sem("act_evacuated"), "dve": sem("dve_evacuated")}
        slot_full = [sem(f"slot_full{s}") for s in range(NSLOT)]
        in_small, in_x, in_tab, in_ck, in_bc, in_ret = (sem(n) for n in
            ("in_small", "in_x", "in_tab", "in_ck", "in_bc", "in_ret"))
        pool_init = sem("pool_init")
        cond_ready = sem("cond_ready")
        mod_ready = sem("mod_ready")
        gain_ready = sem("gain_ready")
        sq_ready = sem("sq_ready")
        rms_inv = sem("rms_inv")
        hm_ready = sem("hm_ready")
        h_ready = sem("h_ready")
        dve_chain, act_chain, pool_chain = sem("dve_chain"), sem("act_chain"), sem("pool_chain")
        rope_pool, rope_done = sem("rope_pool"), sem("rope_done")
        max_ready, a_ready, osq_ready, o_ready, oT_ready, ssq_root = (sem(n) for n in
            ("max_ready", "a_ready", "osq_ready", "o_ready", "oT_ready", "ssq_root"))
        lam_sum, lam_exp, dec_a, dec_b, dec_done = (sem(n) for n in ("lam_sum", "lam_exp", "dec_a", "dec_b", "dec_done"))
        zero_ready, zero_stored = sem("zero_ready"), sem("zero_stored")
        stored_k, stored_v, stored_s, stored_y = (sem(n) for n in ("stored_k", "stored_v", "stored_s", "stored_y"))
        decay_ready, rope_ret, qd_ready, stat_ready, n_ready, gate_pool, ro_ready = (sem(n) for n in
            ("decay_ready", "rope_ret", "qd_ready", "stat_ready", "n_ready", "gate_pool", "ro_ready"))
        M = []
        for l in range(DEPTH):
            M.append({n: sem(f"moe{l}_{n}") for n in (
                "chosen", "routed", "scores", "idx", "sel", "gathered", "xs_act", "xs_dve", "gu", "silu", "gated",
                "T", "aT_act", "aT_dve", "down", "y_act", "y_dve", "stored0", "stored1",
                "o_ranks", "o_sel", "o_gathered", "o_xs", "o_gu", "o_silu", "o_gated", "o_T", "o_aT", "o_down", "o_y",
                "o_stored", "picked", "ytok", "passed")})

        def filled(eng, name):
            eng.wait_ge(ps_filled, job_no[name] + 1)

        def emptied(eng, name):
            who, n = evac_no[name]
            eng.wait_ge(evac[who], n)

        def settle(eng, l):
            eng.sem_inc(M[l]["passed"], 1)

        def bank(name):
            return psum[:, job_no[name] % NB, :]

        def unit_wait(eng, name):
            n = unit_no[name]
            eng.wait_ge(slot_full[n % NSLOT], full_at[n])

        def slot(name):
            return ring[:, unit_no[name] % NSLOT, :]

        def x_written(n):
            return {0: ("x", KT - 1), 1: ("wo", KT - 1), 2: ("y", 0, KT - 1), 3: ("rwo", KT - 1), 4: ("y", 1, KT - 1)}[n]

        block = ctx.enter_context(nc.Block())

        @block.sync
        def _(sp):
            sp.dma_start(base_sb[:, :], base_d).then_inc(in_tab, 16)
            sp.dma_start(xtok[:, 0, :], ins["x_prompt"][0]).then_inc(in_x, 16)
            sp.dma_start(xtok[:, 1:TT, :], ins["x_sample"][0].rearrange("(t p) d -> p t d", p=P)).then_inc(in_x, 16)
            sp.dma_start(rows0[0:96, :], ins["b_ada"].rearrange("l (n p) -> (l n) p", p=P)).then_inc(in_small, 16)
            sp.dma_start(rows0[96:112, :], ins["norm_mix_g"].rearrange("l (n p) -> (l n) p", p=P)).then_inc(in_small, 16)
            sp.dma_start(rows0[112:128, :], ins["norm_ffn_g"].rearrange("l (n p) -> (l n) p", p=P)).then_inc(in_small, 16)
            sp.dma_start(rows1[0:8, :], ins["final_norm_g"].rearrange("(n p) -> n p", p=P)).then_inc(in_small, 16)
            sp.dma_start(rows1[8:16, :], ins["c_ctx"].rearrange("(n p) -> n p", p=P)).then_inc(in_small, 16)
            sp.dma_start(rows1[16:24, :], ins["c"][0].rearrange("(n p) -> n p", p=P)).then_inc(in_small, 16)
            sp.dma_start(rows1[24:25, :], ins["da_subln_g"]).then_inc(in_small, 16)

            def source(name):
                kind = name[0]
                cols = lambda w, a, b: w.rearrange("(k p) n -> p k n", p=P)[:, :, a:b]
                to = slot(name)
                if kind == "ada":
                    _, l, u = name
                    return [(to.rearrange("p (k n) -> p k n", k=KT), cols(ins["w_ada"][l], 512 * u, 512 * u + 512))]
                if kind in "qkv":
                    at = 1024 * "qkv".index(kind) + 512 * name[1]
                    return [(to.rearrange("p (k n) -> p k n", k=KT), cols(ins["da_w_qkv"][0], at, at + 512))]
                if kind == "wo":
                    return [(to.rearrange("p (k n) -> p k n", k=KT), cols(ins["da_w_o"][0], 512 * name[1], 512 * name[1] + 512))]
                if kind == "rqk":
                    v = to.rearrange("p (k s n) -> p k s n", k=KT, s=2)
                    w = ins["ret_w_qkv"][0]
                    return [(v[:, :, s, :], cols(w, 1024 * s + RDK * name[1], 1024 * s + RDK * (name[1] + 1))) for s in range(2)]
                if kind == "rv":
                    return [(to.rearrange("p (k n) -> p k n", k=KT), cols(ins["ret_w_qkv"][0], 2048 + RDV * name[1], 2048 + RDV * (name[1] + 1)))]
                if kind == "rg":
                    w = ins["ret_w_gate_fwd" if name[2] == 0 else "ret_w_gate_bwd"][0]
                    return [(to.rearrange("p (k n) -> p k n", k=KT), cols(w, RDV * name[1], RDV * (name[1] + 1)))]
                if kind == "state":
                    v = to[:, 0:2048].rearrange("p (e k n) -> p e k n", e=2, k=2)
                    return [(v[:, e], ins[w][0, 0, name[1]].rearrange("(k p) n -> p k n", p=P))
                            for e, w in enumerate(("state_ret_fwd", "state_ret_bwd"))]
                if kind == "rwo":
                    return [(to.rearrange("p (k n) -> p k n", k=16), cols(ins["ret_w_o"][0], 256 * name[1], 256 * name[1] + 256))]
                raise ValueError(name)

            def load(name):
                n = unit_no[name]
                if n >= NSLOT:
                    prior, last_job = UNITS[n - NSLOT]
                    if last_job is not None:
                        filled(sp, last_job)
                    else:
                        _, l, k = prior
                        sp.wait_ge(M[l]["down"], NE)
                        sp.wait_ge(M[l]["gu"], NE)
                        sp.wait_ge(M[l]["o_down"], cum_end[l] + 1)
                        settle(sp, l)
                for to, src in source(name):
                    sp.dma_start(to, src).then_inc(slot_full[n % NSLOT], 16)

            cum_end = {}
            for name, _ in UNITS:
                if name[0] != "moe":
                    load(name)
                    if name == ("ada", 0, 3):
                        sp.dma_start(att_tab, att_d).then_inc(in_ck, 16)
                        sp.dma_start(cktok, ins["cache_attn_k"][0, 0].rearrange("t h c d -> t (h c d)")).then_inc(in_ck, 16)
                        sp.dma_start(cvt, ins["cache_attn_v"][0, 0].rearrange("t h d -> t (h d)")).then_inc(in_ck, 16)
                    if name == ("rqk", 0):
                        sp.dma_start(ret_tab, ret_d).then_inc(in_ret, 16)
                        sp.dma_start(dist_tab[:, 0:dist_np.shape[1]], dist_d).then_inc(in_ret, 16)
                    continue
                _, l, k = name
                if k:
                    continue
                m, u0 = M[l], unit_no[("moe", l, 0)]
                wg, wu, wd = ins["moe_w_gate"][l], ins["moe_w_up"][l], ins["moe_w_down"][l]

                def expert_load(k, e):
                    s = (u0 + k) % NSLOT
                    if k < 4:
                        w = (wg, wu)[k % 2][ds(e, 1)].rearrange("o (k p) n -> p (o k) n", p=P)
                        to = ring[:, s, :].rearrange("p (k n) -> p k n", k=KT)
                    else:
                        w = wd[ds(e, 1)].rearrange("o (k p) n -> p (o k) n", p=P)
                        to = ring[:, s, :].rearrange("p (k n) -> p k n", k=4)
                    sp.dma_start(to, w).then_inc(slot_full[s], 16)

                for k in range(6):
                    filled(sp, UNITS[u0 + k - NSLOT][1])
                    expert_load(k, (0, 0, 1, 1, 0, 1)[k])
                sp.wait_ge(m["routed"], 1)
                with sp.Fori(1, NE // 2) as q:
                    ovA = sp.value_load(RT[l][0:1, ds(2 * q - 1, 1)], min_val=0, max_val=MAXOV)
                    ovB = sp.value_load(RT[l][0:1, ds(2 * q, 1)], min_val=0, max_val=MAXOV)
                    sp.wait_ge(m["gu"], 2 * q - 1)
                    settle(sp, l)
                    sp.wait_ge(m["o_down"], ovA + 1)
                    settle(sp, l)
                    expert_load(0, 2 * q)
                    expert_load(1, 2 * q)
                    sp.wait_ge(m["gu"], 2 * q)
                    settle(sp, l)
                    sp.wait_ge(m["o_down"], ovB + 1)
                    settle(sp, l)
                    expert_load(2, 2 * q + 1)
                    expert_load(3, 2 * q + 1)
                    sp.wait_ge(m["down"], 2 * q - 1)
                    settle(sp, l)
                    expert_load(4, 2 * q)
                    sp.wait_ge(m["down"], 2 * q)
                    settle(sp, l)
                    expert_load(5, 2 * q + 1)
                cum_end[l] = sp.value_load(RT[l][0:1, NE:NE + 1], min_val=0, max_val=MAXOV)

        @block.tensor
        def _(pe):
            cursor = [0]

            def open_job(name):
                n = cursor[0]
                assert JOBS[n][0] == name, (JOBS[n], name)
                if n >= NB:
                    emptied(pe, JOBS[n - NB][0])
                cursor[0] += 1
                return psum[:, n % NB, :]

            def done(ins_):
                ins_.then_inc(ps_filled, 1)

            mm, tr = nc.tensor.matmul, nc.tensor.transpose

            pe.wait_ge(in_tab, 16)
            pe.wait_ge(in_small, 16 * 7)
            b = open_job(("small", 0))
            done(tr(b[:, 0:P], rows0[:, :], ident))
            b = open_job(("small", 1))
            done(tr(b[:, 0:25], rows1[0:25, :], ident[0:25, 0:25]))
            pe.wait_ge(in_x, 32)
            for kt in range(KT):
                b = open_job(("x", kt))
                for t in range(TT):
                    last = tr(b[:, P * t:P * t + P], xtok[:, t, P * kt:P * kt + P], ident)
                done(last)

            def ada(layer, units):
                def turn(u, n):
                    emptied(pe, ("ada", layer, u))
                    b = open_job(("adaT", layer, u))
                    for f in range(4):
                        last = tr(b[:, P * f:P * f + P], ada_rows[:, ada_at[(layer, u)], P * f:P * f + P], ident)
                    done(last)

                for n, u in enumerate(units):
                    unit_wait(pe, ("ada", layer, u))
                    w = slot(("ada", layer, u)).rearrange("p (k n) -> p k n", k=KT)
                    b = open_job(("ada", layer, u))
                    for kt in range(KT):
                        j = kt % 4
                        last = mm(b[32 * j:32 * j + 32, :], cond[:, kt, :], w[:, kt, :], start=kt < 4, stop=kt >= 4)
                    done(last)
                    if n:
                        turn(units[n - 1], n - 1)
                turn(units[-1], 0)

            def norm(n):
                b = open_job(("norm", n))
                for kt in range(KT):
                    pe.wait_ge(sq_ready, KT * n + kt + 1)
                    last = mm(b[:, 0:TOK], ones[:, :], sq[:, kt, :], start=kt == 0, stop=kt == KT - 1)
                done(last)

            def to_features(name, w, col, h_from=None):
                b = open_job(name)
                for kt in range(KT):
                    if h_from is not None:
                        pe.wait_ge(h_ready, h_from + kt + 1)
                    last = mm(b[:, 0:TOK], w[:, kt, col:col + P], hT[:, kt, :], start=kt == 0, stop=kt == KT - 1)
                done(last)

            def to_tokens(name, w, t):
                b = open_job(name)
                for kt in range(KT):
                    last = mm(b, hT[:, kt, P * t:P * t + P], w[:, kt, :], start=kt == 0, stop=kt == KT - 1)
                done(last)

            pe.wait_ge(pool_init, 2)
            pe.wait_ge(cond_ready, 2)
            ada(0, range(4))
            norm(0)
            pe.wait_ge(in_ck, 48)
            for i in range(2):
                b = open_job(("ck", i))
                for j in range(4):
                    c = P * (4 * i + j)
                    last = tr(b[:, P * j:P * j + P], cktok[:, c:c + P], ident)
                done(last)

            swap = table(att_tab, att_at, "swap")
            n_rope = 0
            for g in range(2):
                for kind in "qk":
                    unit_wait(pe, (kind, g))
                    w = slot((kind, g)).rearrange("p (k n) -> p k n", k=KT)

                    def partner(h, n):
                        emptied(pe, (kind, h))
                        b = open_job((kind + "swap", h))
                        done(mm(b[:, 0:NS_TOK], swap, raw[:, n % 2, NP_TOK:TOK], start=True, stop=True))

                    for i in range(HALF):
                        to_features((kind, HALF * g + i), w, P * i, 0 if n_rope == 0 else None)
                        if i:
                            partner(HALF * g + i - 1, n_rope - 1)
                        n_rope += 1
                    partner(HALF * g + HALF - 1, n_rope - 1)
                pe.wait_ge(rope_pool, n_rope)
                b = open_job(("knew", g))
                for i in range(HALF):
                    last = tr(b[:, P * i:P * i + P], kT[:, i, 0:P], ident)
                done(last)
                unit_wait(pe, ("v", g))
                w = slot(("v", g)).rearrange("p (k n) -> p k n", k=KT)
                for t in range(TT):
                    to_tokens(("v", g, t), w, t)
                pe.wait_ge(rope_done, n_rope)
                for i in range(HALF + 2):
                    h = HALF * g + i
                    if i < HALF:
                        for r in range(TT):
                            for c in range(2):
                                b = open_job(("S", h, r, c))
                                q = qz[:, c, i, P * r:P * r + P]
                                if r == 0:
                                    done(mm(b[:, 0:P], q, kT[:, i, 0:P], start=True, stop=True))
                                else:
                                    mm(b[:, 0:P], q, ckT[:, h, :], start=True, stop=True)
                                    done(mm(b[:, P:TOK], q, kT[:, i, P:TOK], start=True, stop=True))
                    if 1 <= i <= HALF:
                        for r in range(TT):
                            pe.wait_ge(a_ready, TT * (h - 1) + r + 1)
                            b = open_job(("aT", h - 1, r))
                            for k in range(1 if r == 0 else 3):
                                last = tr(b[:, P * k:P * k + P], aw[:, r, P * k:P * k + P], ident)
                            done(last)
                        emptied(pe, ("aT", h - 1, TT - 1))
                        if i == 1:
                            emptied(pe, ("v", g, TT - 1))
                        b = open_job(("o", h - 1))
                        vh = slice(P * (i - 1), P * i)
                        mm(b[:, 0:P], vtok[:, 0, vh], aTp, start=True, stop=True)
                        mm(b[:, P:TOK], cvt[:, P * (h - 1):P * h], aTs[:, 0, :], start=True, stop=False)
                        mm(b[:, P:TOK], vtok[:, 1, vh], aTs[:, 1, :], start=False, stop=False)
                        done(mm(b[:, P:TOK], vtok[:, 2, vh], aTs[:, 2, :], start=False, stop=True))
                    if i >= 2:
                        pe.wait_ge(osq_ready, h - 1)
                        b = open_job(("oss", h - 2))
                        done(mm(b[:, 0:TOK], ones[:, :], osq[:, (h - 2) % 2, :], start=True, stop=True))
            ada(0, range(4, 12))
            ada(1, range(12))
            pe.wait_ge(oT_ready, 2)
            for ft in range(KT):
                if ft % 4 == 0:
                    unit_wait(pe, ("wo", ft // 4))
                w = slot(("wo", ft // 4)).rearrange("p (k n) -> p k n", k=KT)
                b = open_job(("wo", ft))
                for h in range(HEADS):
                    last = mm(b[:, 0:TOK], w[:, h, P * (ft % 4):P * (ft % 4) + P], oT[:, h, :], start=h == 0, stop=h == HEADS - 1)
                done(last)

            def experts(l):
                m = M[l]
                norm(2 * l + 1)
                b = open_job(("logit", l))
                for kt in range(KT):
                    pe.wait_ge(h_ready, KT * (2 * l + 1) + kt + 1)
                    last = mm(b[0:NE, 0:TOK], wr[:, kt, :], hT[:, kt, :], start=kt == 0, stop=kt == KT - 1)
                done(last)
                emptied(pe, ("logit", l))
                b = open_job(("logitT", l))
                for t in range(TT):
                    last = tr(b[:, NE * t:NE * t + NE], wm["lg"][0:NE, P * t:P * t + P], ident[0:NE, 0:NE])
                done(last)
                for i in range(2 * TT):
                    b = open_job(("htok", l, i))
                    for j in range(4):
                        last = tr(b[:, P * j:P * j + P], hT[:, 4 * (i % 2) + j, P * (i // 2):P * (i // 2) + P], ident)
                    done(last)
                pe.wait_ge(m["chosen"], 1)
                b = open_job(("rank", l))
                Mt = v3("M", TT)
                for t in range(TT):
                    for s in range(t + 1):
                        mm(b[:, NE * t:NE * t + NE], before if s == t else ones[:, :], Mt[:, s, :], start=s == 0, stop=s == t)
                for s in range(TT):
                    last = mm(b[:, NE * TT:NE * TT + NE], ones[:, :], Mt[:, s, :], start=s == 0, stop=s == TT - 1)
                done(last)

                u0 = unit_no[("moe", l, 0)]
                for n in range(2 * TT):
                    emptied(pe, ("htok", l, n))
                emptied(pe, ("rank", l))
                pe.wait_ge(m["routed"], 1)

                def gather(pair, par):
                    pe.wait_ge(m["sel"], pair + 1)
                    for kt in range(KT):
                        out = psum[:, 2 + kt // 4, P * (kt % 4):P * (kt % 4) + P]
                        for t in range(TT):
                            last = mm(out, htok[:, t, P * kt:P * kt + P], sel[:, t].rearrange("p x s -> p (x s)"),
                                      start=t == 0, stop=t == TT - 1)
                    last.then_inc(m["gathered"], 1)

                def unit(q, k):
                    n = u0 + k
                    pe.wait_ge(slot_full[n % NSLOT], q * 16 + full_at[n])
                    return ring[:, n % NSLOT, :]

                def overflow(e, x, wg, wu, q):
                    lo = pe.value_load(RT[l][0:1, ds(e, 1)], min_val=0, max_val=MAXOV)
                    hi = pe.value_load(RT[l][0:1, ds(e + 1, 1)], min_val=0, max_val=MAXOV)
                    ov = psum[:, 7, :]
                    with pe.If(lo < hi):
                        wd = unit(q, 4 + x).rearrange("p (k n) -> p k n", k=4)
                        settle(pe, l)
                        with pe.Fori(lo, hi) as o:
                            pe.wait_ge(m["o_sel"], o + 1)
                            for kt in range(KT):
                                for t in range(TT):
                                    last = mm(ov[:, BLK * kt:BLK * kt + BLK], htok[:, t, P * kt:P * kt + P], osel[:, t, :],
                                              start=t == 0, stop=t == TT - 1)
                            last.then_inc(m["o_gathered"], 1)
                            pe.wait_ge(m["o_xs"], o + 1)
                            for kt in range(KT):
                                mm(ov[0:BLK, :], ox[:, kt, :], wg[:, kt, :], start=kt == 0, stop=kt == KT - 1)
                                last = mm(ov[BLK:P, :], ox[:, kt, :], wu[:, kt, :], start=kt == 0, stop=kt == KT - 1)
                            last.then_inc(m["o_gu"], 1)
                            pe.wait_ge(m["o_gated"], o + 1)
                            settle(pe, l)
                            for k in range(4):
                                last = tr(ov[:, BLK * k:BLK * k + BLK], oa[0:BLK, P * k:P * k + P], ident[0:BLK, 0:BLK])
                            last.then_inc(m["o_T"], 1)
                            pe.wait_ge(m["o_aT"], o + 1)
                            for k in range(4):
                                mm(ov[0:BLK, :], oaT[:, k, :], wd[:, k, 0:512], start=k == 0, stop=k == 3)
                                last = mm(ov[BLK:P, :], oaT[:, k, :], wd[:, k, 512:D], start=k == 0, stop=k == 3)
                            last.then_inc(m["o_down"], 1)

                gather(0, 0)
                with pe.Fori(0, NE // 4) as it:
                    for par in range(2):
                        q = it * 2 + par
                        pe.wait_ge(m["xs_act"], q + 1)
                        pe.wait_ge(m["xs_dve"], q + 1)
                        for x in range(2):
                            e = q * 2 + x
                            wg = unit(q, 2 * x).rearrange("p (k n) -> p k n", k=KT)
                            wu = unit(q, 2 * x + 1).rearrange("p (k n) -> p k n", k=KT)
                            pe.wait_ge(m["gated"], e + 1)
                            for kt in range(KT):
                                xk = xs[:, par, kt, BLK * x:BLK * x + BLK]
                                mm(psum[0:BLK, x, :], xk, wg[:, kt, :], start=kt == 0, stop=kt == KT - 1)
                                last = mm(psum[BLK:P, x, :], xk, wu[:, kt, :], start=kt == 0, stop=kt == KT - 1)
                            last.then_inc(m["gu"], 1)
                            overflow(e, x, wg, wu, q)
                        gather(q + 1, 1 - par)
                        for x in range(2):
                            e = q * 2 + x
                            pe.wait_ge(m["gated"], e + 3)
                            settle(pe, l)
                            for k in range(4):
                                last = tr(psum[:, x, BLK * k:BLK * k + BLK], ea[0:BLK, x, P * k:P * k + P],
                                          ident[0:BLK, 0:BLK])
                            last.then_inc(m["T"], 1)
                        for x in range(2):
                            wd = unit(q, 4 + x).rearrange("p (k n) -> p k n", k=4)
                            pe.wait_ge(m["aT_act" if x == 0 else "aT_dve"], q + 1)
                            pe.wait_ge(m["y_act" if x == 0 else "y_dve"], q + 1)
                            for k in range(4):
                                mm(psum[0:BLK, 5 + x, :], eaT[:, x, k, :], wd[:, k, 0:512], start=k == 0, stop=k == 3)
                                last = mm(psum[BLK:P, 5 + x, :], eaT[:, x, k, :], wd[:, k, 512:D], start=k == 0, stop=k == 3)
                            last.then_inc(m["down"], 1)
                pe.wait_ge(m["ytok"], TT)
                for ft in range(KT):
                    b = open_job(("y", l, ft))
                    for t in range(TT):
                        last = tr(b[:, P * t:P * t + P], ytok[:, t, P * ft:P * ft + P], ident)
                    done(last)

            experts(0)

            norm(2)
            for h in range(RH):
                unit_wait(pe, ("rqk", h))
                w = slot(("rqk", h)).rearrange("p (k n) -> p k n", k=KT)
                for t in range(2):
                    to_features(("rq", h, t), w, P * t, KT * 2 if h == 0 and t == 0 else None)
                for t in range(2):
                    to_features(("rk", h, t), w, RDK + P * t)

                def turn_o(hh):
                    for t in range(TT):
                        pe.wait_ge(ro_ready, TT * hh + t + 1)
                        b = open_job(("roT", hh, t))
                        for f in range(4):
                            last = tr(b[:, P * f:P * f + P], ro[:, t, P * f:P * f + P], ident)
                        done(last)

                unit_wait(pe, ("rv", h))
                w = slot(("rv", h)).rearrange("p (k n) -> p k n", k=KT)
                for t in range(TT):
                    to_tokens(("rv", h, t), w, t)
                for d in range(2):
                    unit_wait(pe, ("rg", h, d))
                    w = slot(("rg", h, d)).rearrange("p (k n) -> p k n", k=KT)
                    for t in range(TT):
                        to_tokens(("rg", h, d, t), w, t)
                if h:
                    turn_o(h - 1)
                pe.wait_ge(rope_ret, 2 * h + 2)
                b = open_job(("rkT", h))
                for t in range(2):
                    last = tr(b[:, P * t:P * t + P], rk[:, t, 0:P], ident)
                done(last)
                b = open_job(("rA", h, 0))
                for t in range(2):
                    mm(b[:, 0:P], rk[:, t, 0:P], rq[:, t, 0:P], start=t == 0, stop=t == 1)
                for t in range(2):
                    last = mm(b[:, P:TOK], rk[:, t, P:2 * P], rq[:, t, P:TOK], start=t == 0, stop=t == 1)
                done(last)
                b = open_job(("rA", h, 1))
                for t in range(2):
                    last = mm(b[:, 0:NS_TOK], rk[:, t, 2 * P:TOK], rq[:, t, P:TOK], start=t == 0, stop=t == 1)
                done(last)
                emptied(pe, ("rkT", h))
                for d in range(2):
                    for t in range(2):
                        b = open_job(("rs", h, d, t))
                        done(mm(b, kd[:, d, P * t:P * t + P], rv[:, 0, :], start=True, stop=True))
                unit_wait(pe, ("state", h))
                S0 = slot(("state", h))[:, 0:2048].rearrange("p (e k n) -> p e k n", e=2, k=2)
                emptied(pe, ("rA", h, 1))
                pe.wait_ge(qd_ready, 2 * h + 2)
                for t in range(TT):
                    for d in range(2):
                        b = open_job(("ro", h, t, d))
                        if t == 0:
                            terms = [(rA[:, d, 0:P], rv[:, 0, :])]
                        elif d == 0:
                            terms = [(rA[:, 0, P * t:P * t + P], rv[:, 1, :])] + ([(rA[:, 0, 3 * P:4 * P], rv[:, 2, :])] if t == 2 else [])
                        else:
                            terms = ([(rA[:, 1, P:2 * P], rv[:, 1, :])] if t == 1 else []) + [(rA[:, 1, P * (t + 1):P * (t + 2)], rv[:, 2, :])]
                        if t:
                            terms += [(qd[:, d, k, P * (t - 1):P * t], S0[:, d, k, :]) for k in range(2)]
                        for n, (a, v) in enumerate(terms):
                            last = mm(b, a, v, start=n == 0, stop=n == len(terms) - 1)
                        done(last)
            turn_o(RH - 1)
            emptied(pe, ("roT", RH - 1, TT - 1))
            for ft in range(KT):
                if ft % 2 == 0:
                    unit_wait(pe, ("rwo", ft // 2))
                w = slot(("rwo", ft // 2)).rearrange("p (k n) -> p k n", k=16)
                b = open_job(("rwo", ft))
                for k in range(16):
                    last = mm(b[:, 0:TOK], w[:, k, P * (ft % 2):P * (ft % 2) + P], roT(k), start=k == 0, stop=k == 15)
                done(last)
            experts(1)
            norm(4)
            for i in range(2 * TT):
                b = open_job(("yout", i))
                for j in range(4):
                    pe.wait_ge(hm_ready, KT * 4 + 4 * (i % 2) + j + 1)
                    last = tr(b[:, P * j:P * j + P], hT[:, 4 * (i % 2) + j, P * (i // 2):P * (i // 2) + P], ident)
                done(last)
            assert cursor[0] == len(JOBS)

        @block.scalar
        def _(act):
            chain = [0]
            A = nc.scalar.activation

            def link(ins_):
                chain[0] += 1
                ins_.then_inc(act_chain, 1)
                act.wait_ge(act_chain, chain[0])

            act.wait_ge(zero_ready, 1)
            for n in range(MAXOV * BLK // P):
                r = NE * BLK + P * n
                act.dma_start(scratch[r:r + P, :], zrow).then_inc(zero_stored, 16)
            act.wait_ge(in_bc, 16 * 8)
            emptied(act, ("small", 1))
            act.wait_ge(pool_init, 2)
            A(cond[:, :, 0:1], cols1[:, 8:16].unsqueeze(2), ACT.Silu).then_inc(cond_ready, 1)
            A(cond[:, :, 1:2], cols1[:, 16:24].unsqueeze(2), ACT.Silu).then_inc(cond_ready, 1)

            def ada(layer, units):
                for u in units:
                    filled(act, ("ada", layer, u))
                    A(ada_rows[:, ada_at[(layer, u)], :], bank(("ada", layer, u)), ACT.Copy).then_inc(evac["act"], 1)

            def norm(n):
                emptied(act, x_written(n))
                for kt in range(KT):
                    A(sq[:, kt, :], xT[:, kt, :], ACT.Square).then_inc(sq_ready, 1)
                filled(act, ("norm", n))
                A(rms[:, :], bank(("norm", n))[:, 0:TOK], ACT.Sqrt, bias=eps[:, :], scale=1.0 / D).then_inc(evac["act"], 1)
                if n == 4:
                    return
                l, part = n // 2, 3 * (n % 2)
                for kt in range(KT):
                    act.wait_ge(hm_ready, KT * n + kt + 1)
                    for c, a, z in SEG:
                        last = A(hT[:, kt, a:z], hT[:, kt, a:z], ACT.Identity, bias=mod[:, l, 8 * part + kt, c:c + 1])
                    last.then_inc(h_ready, 1)

            ada(0, range(4))
            act.wait_ge(lam_sum, 1)
            A(lam_s[:, 2:4], lam_s[:, 0:2], ACT.Exp).then_inc(lam_exp, 1)
            act.wait_ge(dec_a, 1)
            link(A(dec[:, 2, :], dec[:, 1, :], ACT.Exp))
            A(dec[:, 3, :], dec[:, 2, :], ACT.Ln, bias=ones[:, 0:1]).then_inc(dec_b, 1)
            norm(0)
            for i in range(2):
                filled(act, ("ck", i))
                A(wa["ck"][:, 512 * i:512 * i + 512], bank(("ck", i)), ACT.Copy).then_inc(evac["act"], 1)
            n_rope = 0
            for g in range(2):
                for kind in "qk":
                    for i in range(HALF):
                        h = HALF * g + i
                        filled(act, (kind, h))
                        if n_rope >= 2:
                            act.wait_ge(rope_pool, n_rope - 1)
                            act.wait_ge(rope_done, n_rope - 1)
                        A(raw[:, n_rope % 2, :], bank((kind, h))[:, 0:TOK], ACT.Copy,
                          scale=HD ** -0.5 if kind == "q" else 1.0).then_inc(evac["act"], 1)
                        n_rope += 1
                filled(act, ("knew", g))
                if g:
                    act.wait_ge(oT_ready, 1)
                A(ko, bank(("knew", g)), ACT.Copy).then_inc(evac["act"], 1)
                emptied(act, ("knew", g))
                act.dma_start(new_k[0, 0, :, HALF * g:HALF * g + HALF].rearrange("t h c d -> t (h c d)"), ko).then_inc(stored_k, 16)
                for t in range(TT):
                    filled(act, ("v", g, t))
                    if g and t == 0:
                        act.wait_ge(stored_v, 16)
                    A(vtok[:, t, :], bank(("v", g, t)), ACT.Copy).then_inc(evac["act"], 1)
                    if t == 0:
                        emptied(act, ("v", g, 0))
                        act.dma_start(new_v[0, 0, :, HALF * g:HALF * g + HALF].rearrange("t h d -> t (h d)"), vtok[:, 0, :]).then_inc(stored_v, 16)
                for i in range(HALF + 2):
                    h = HALF * g + i
                    if i < HALF:
                        for r in range(TT):
                            n = TT * h + r
                            w = P if r == 0 else TOK
                            for c in range(2):
                                act.wait_ge(max_ready, 2 * n + c + 1)
                                if n >= 2 and c == 0:
                                    act.wait_ge(a_ready, n - 1)
                                A(pr[:, n % 2, c, 0:w], bank(("S", h, r, c))[:, 0:w], ACT.Exp, bias=nm[:, n % 6, c:c + 1],
                                  accum_out=sm[:, n % 6, c:c + 1]).then_inc(evac["act"], 1)
                    if 1 <= i <= HALF:
                        for r in range(TT):
                            filled(act, ("aT", h - 1, r))
                            if h > 1 and r == 0:
                                filled(act, ("o", h - 2))
                            if r == 0:
                                A(aTp, bank(("aT", h - 1, r))[:, 0:P], ACT.Copy).then_inc(evac["act"], 1)
                            else:
                                A(aTs[:, :, P * (r - 1):P * r], bank(("aT", h - 1, r))[:, 0:TOK].rearrange("p (k t) -> p k t", k=3),
                                  ACT.Copy).then_inc(evac["act"], 1)
                        emptied(act, ("o", h - 1))
                        if h - 1 >= 2:
                            filled(act, ("oss", h - 3))
                        A(osq[:, (h - 1) % 2, :], oT[:, h - 1, :], ACT.Square).then_inc(osq_ready, 1)
                emptied(act, ("oss", HALF * g + HALF - 1))
                A(ss[:, :, :], ss[:, :, :], ACT.Sqrt, bias=eps[:, :], scale=1.0 / HV).then_inc(ssq_root, 1)
            ada(0, range(4, 12))
            ada(1, range(12))

            def experts(l):
                m = M[l]
                if l == 0:
                    act.wait_ge(stored_k, 32)
                    act.wait_ge(stored_v, 32)
                else:
                    act.wait_ge(stored_s, 16 * 4 * RH)
                norm(2 * l + 1)
                filled(act, ("logitT", l))
                A(wm["s"], bank(("logitT", l))[:, 0:TT * NE], ACT.Sigmoid).then_inc(evac["act"], 1)
                for i in range(1, 2 * TT, 2):
                    filled(act, ("htok", l, i))
                    A(htok[:, i // 2, 512 * (i % 2):512 * (i % 2) + 512], bank(("htok", l, i)), ACT.Copy).then_inc(evac["act"], 1)
                act.sem_inc(m["y_act"], 1)
                act.sem_inc(m["stored0"], 32)
                act.sem_inc(m["stored1"], 32)
                act.sem_inc(m["o_stored"], 32)
                act.wait_ge(m["routed"], 1)

                def take_xs(pair, par):
                    act.wait_ge(m["gathered"], pair + 1)
                    A(xs[:, par, 0:4, :].rearrange("p k s -> p (k s)"), psum[:, 2, :], ACT.Copy).then_inc(m["xs_act"], 1)

                def overflow(e):
                    lo = act.value_load(RT[l][0:1, ds(e, 1)], min_val=0, max_val=MAXOV)
                    hi = act.value_load(RT[l][0:1, ds(e + 1, 1)], min_val=0, max_val=MAXOV)
                    with act.If(lo < hi):
                        with act.Fori(lo, hi) as o:
                            act.wait_ge(m["o_gu"], o + 1)
                            A(osg[BLK:P, :], psum[0:BLK, 7, :], ACT.Silu).then_inc(m["o_silu"], 1)
                            act.wait_ge(m["o_y"], o + 1)
                            for s in range(2):
                                act.dma_start(scratch[ds(o * BLK + NE * BLK, BLK), 512 * s:512 * s + 512],
                                              oy[BLK * s:BLK * s + BLK, :]).then_inc(m["o_stored"], 16)

                take_xs(0, 0)
                with act.Fori(0, NE // 4) as it:
                    for par in range(2):
                        q = it * 2 + par
                        for x in range(2):
                            e = q * 2 + x
                            act.wait_ge(m["gu"], e + 1)
                            A(sg[BLK:P, x, :], psum[0:BLK, x, :], ACT.Silu).then_inc(m["silu"], 1)
                            overflow(e)
                        take_xs(q + 1, 1 - par)
                        act.wait_ge(m["T"], q * 2 + 1)
                        A(eaT[:, 0].rearrange("p k s -> p (k s)"), psum[:, 0, 0:256], ACT.Copy).then_inc(m["aT_act"], 1)
                        act.wait_ge(m["down"], q * 2 + 1)
                        act.wait_ge(m["stored0"], q * 32 + 32)
                        A(ysb[:, 0, :], psum[:, 5, :], ACT.Copy).then_inc(m["y_act"], 1)
                        for x in range(2):
                            act.wait_ge(m["y_act" if x == 0 else "y_dve"], q + 2)
                            for s in range(2):
                                act.dma_start(scratch[ds(q * 2 * BLK + x * BLK, BLK), 512 * s:512 * s + 512],
                                              ysb[BLK * s:BLK * s + BLK, x, :]).then_inc(m[f"stored{x}"], 16)

            experts(0)

            def turned(hh):
                for t in range(TT):
                    filled(act, ("roT", hh, t))
                    for f in range(4):
                        last = A(roT(4 * hh + f)[:, P * t:P * t + P], bank(("roT", hh, t))[:, P * f:P * f + P], ACT.Copy)
                    last.then_inc(evac["act"], 1)

            norm(2)
            act.wait_ge(in_ret, 32)
            act.wait_ge(dec_done, 1)
            for h in range(RH):
                for j, (kind, to) in enumerate((("rq", rq), ("rk", rk))):
                    if h:
                        filled(act, ("ro", h - 1, TT - 1, 1))
                        act.wait_ge(qd_ready, 2 * h)
                    for t in range(2):
                        filled(act, (kind, h, t))
                        A(to[:, t, :], bank((kind, h, t))[:, 0:TOK], ACT.Copy,
                          scale=1.0 if kind == "rq" else RDK ** -0.5).then_inc(evac["act"], 1)
                dt_ = lambda n: table(dist_tab, dist_at, n)
                for d, s in enumerate("fb"):
                    lg = dec[:, 5, RH * d + h:RH * d + h + 1]
                    A(rE[:, d, 0:NS_TOK + 1], dt_(f"rel_{s}"), ACT.Exp, scale=lg).then_inc(decay_ready, 1)
                    A(qe[:, d, :], dt_(f"q_{s}"), ACT.Exp, scale=lg).then_inc(decay_ready, 1)
                if h:
                    act.wait_ge(gate_pool, TT * h)
                    act.wait_ge(ro_ready, TT * h)
                for d in range(2):
                    for t in range(TT):
                        filled(act, ("rg", h, d, t))
                        A(rg[:, d, t, :], bank(("rg", h, d, t)), ACT.Silu).then_inc(evac["act"], 1)
                if h:
                    turned(h - 1)
                for d in range(2):
                    for t in range(2):
                        n = 4 * h + 2 * d + t
                        filled(act, ("rs", h, d, t))
                        if n:
                            act.wait_ge(stored_s, 16 * n)
                        A(st, bank(("rs", h, d, t)), ACT.Copy).then_inc(evac["act"], 1)
                        emptied(act, ("rs", h, d, t))
                        act.dma_start((new_sf if d == 0 else new_sb)[0, 0, h, P * t:P * t + P, :], st).then_inc(stored_s, 16)
                for t in range(TT):
                    act.wait_ge(stat_ready, TT * h + t + 1)
                    if TT * h + t >= 1:
                        act.wait_ge(gate_pool, TT * h + t)
                        act.wait_ge(ro_ready, TT * h + t)
                    for d in range(2):
                        A(rn[:, d, :], bank(("ro", h, t, d)), ACT.Identity, bias=nw[:, 12 + d:13 + d], scale=nw[:, 2 + d:3 + d]).then_inc(evac["act"], 1)
            turned(RH - 1)
            experts(1)
            norm(4)
            n = 0
            for i in range(1, 2 * TT, 2):
                filled(act, ("yout", i))
                A(yo(i), bank(("yout", i)), ACT.Copy).then_inc(evac["act"], 1)
            for i in range(2 * TT):
                emptied(act, ("yout", i))
                t, half = i // 2, i % 2
                dst = (y_prompt[0] if t == 0 else y_sample[0, P * (t - 1):P * t])[:, 512 * half:512 * half + 512]
                act.dma_start(dst, yo(i)).then_inc(stored_y, 16)
            act.wait_ge(stored_y, 16 * 2 * TT)

        @block.vector
        def _(dve):
            chain = [0]
            V = nc.vector

            def link(ins_):
                chain[0] += 1
                ins_.then_inc(dve_chain, 1)
                dve.wait_ge(dve_chain, chain[0])

            V.memset(eps[:, :], EPS)
            filled(dve, ("small", 0))
            V.tensor_copy(cols0[:, :], bank(("small", 0))[:, 0:P]).then_inc(evac["dve"], 1)
            filled(dve, ("small", 1))
            V.tensor_copy(cols1[:, :], bank(("small", 1))[:, 0:25]).then_inc(evac["dve"], 1)
            for kt in range(KT):
                filled(dve, ("x", kt))
                V.tensor_copy(xT[:, kt, :], bank(("x", kt))[:, 0:TOK]).then_inc(evac["dve"], 1)
            dve.wait_ge(in_bc, 16 * 8)
            link(V.tensor_tensor(lam_p[:, 0, :], lamrow[:, 0, :], lamrow[:, 1, :], ALU.mult))
            link(V.tensor_tensor(lam_p[:, 1, :], lamrow[:, 2, :], lamrow[:, 3, :], ALU.mult))
            V.tensor_reduce(out=lam_s[:, 0:2], in_=lam_p[:, :, :], axis=AX.X, op=ALU.add).then_inc(lam_sum, 1)
            link(V.tensor_scalar(dec[:, 4, :], dec[:, 0, :], -1.0, None, ALU.mult))
            V.tensor_tensor(dec[:, 1, :], dec[:, 0, :], dec[:, 4, :], ALU.min).then_inc(dec_a, 1)
            emptied(dve, ("small", 1))
            link(V.tensor_scalar(subg[:, :], cols1[:, 24:25], 1.0 - LAM_INIT, None, ALU.mult))
            dve.wait_ge(lam_exp, 1)
            link(V.tensor_tensor(lam_s[:, 0:1], lam_s[:, 3:4], lam_s[:, 2:3], ALU.subtract))
            link(V.tensor_scalar(lam_s[:, 0:1], lam_s[:, 0:1], -LAM_INIT, None, ALU.add))
            dve.wait_ge(dec_b, 1)
            link(V.tensor_scalar(dec[:, 4, :], dec[:, 0, :], 0.0, None, ALU.min))
            V.tensor_tensor(dec[:, 5, :], dec[:, 4, :], dec[:, 3, :], ALU.subtract).then_inc(dec_done, 1)

            def ada(layer, units):
                for u in units:
                    filled(dve, ("adaT", layer, u))
                    src = bank(("adaT", layer, u)).rearrange("p (f j r) -> p f r j", f=4, j=4)[:, :, 0:2, :]
                    part = mod[:, layer, 4 * u:4 * u + 4, :]
                    V.tensor_reduce(out=part, in_=src, axis=AX.X, op=ALU.add).then_inc(evac["dve"], 1)
                    emptied(dve, ("adaT", layer, u))
                    bias = cols0[:, 48 * layer + 4 * u:48 * layer + 4 * u + 4].unsqueeze(2).broadcast_to([P, 4, 2])
                    V.tensor_tensor(part, part, bias, ALU.add).then_inc(mod_ready, 1)
                    mods[0] += 1
                    if u % 6 == 3:
                        dve.wait_ge(mod_ready, mods[0])
                        s = u // 6
                        g = cols0[:, 96 + 16 * s + 8 * layer:104 + 16 * s + 8 * layer].unsqueeze(2).broadcast_to([P, KT, 2])
                        V.scalar_tensor_tensor(out=gain[:, layer, s], in0=mod[:, layer, 24 * s + 8:24 * s + 16, :], scalar=1.0,
                                               in1=g, op0=ALU.add, op1=ALU.mult).then_inc(gain_ready, 1)

            mods = [0]

            def norm(n):
                if n < 4:
                    dve.wait_ge(gain_ready, n + 1 if n == 0 else 4)
                emptied(dve, ("norm", n))
                V.reciprocal(rinv[:, :], rms[:, :]).then_inc(rms_inv, 1)
                dve.wait_ge(rms_inv, n + 1)
                for kt in range(KT):
                    if n == 4:
                        last = V.scalar_tensor_tensor(out=hT[:, kt, :], in0=xT[:, kt, :], scalar=cols1[:, kt:kt + 1],
                                                      in1=rinv[:, :], op0=ALU.mult, op1=ALU.mult)
                    else:
                        for c, a, z in SEG:
                            last = V.scalar_tensor_tensor(out=hT[:, kt, a:z], in0=xT[:, kt, a:z], scalar=gain[:, n // 2, n % 2, kt, c:c + 1],
                                                          in1=rinv[:, a:z], op0=ALU.mult, op1=ALU.mult)
                    last.then_inc(hm_ready, 1)

            def residual(name, ft, layer, part):
                filled(dve, name)
                for c, a, z in SEG:
                    last = V.scalar_tensor_tensor(out=xT[:, ft, a:z], in0=bank(name)[:, a:z], scalar=mod[:, layer, 8 * part + ft, c:c + 1],
                                                  in1=xT[:, ft, a:z], op0=ALU.mult, op1=ALU.add)
                last.then_inc(evac["dve"], 1)

            ada(0, range(4))
            dve.wait_ge(zero_stored, 16 * (MAXOV * BLK // P))
            norm(0)
            cos, sin = table(att_tab, att_at, "cos"), table(att_tab, att_at, "sin")
            dve.wait_ge(in_ck, 48)
            n_rope = 0
            for g in range(2):
                for kind in "qk":
                    for i in range(HALF):
                        h = HALF * g + i
                        filled(dve, (kind + "swap", h))
                        if n_rope:
                            dve.wait_ge(rope_done, n_rope)
                        V.tensor_tensor(t2, bank((kind + "swap", h))[:, 0:NS_TOK], sin, ALU.mult).then_inc(evac["dve"], 1)
                        emptied(dve, (kind + "swap", h))
                        dve.wait_ge(rope_pool, n_rope + 1)
                        if kind == "q":
                            for c in range(2):
                                s = slice(64 * c, 64 * c + 64)
                                V.tensor_copy(qz[s, c, i, 0:NP_TOK], raw[s, n_rope % 2, 0:NP_TOK])
                                last = V.tensor_tensor(qz[s, c, i, NP_TOK:TOK], t1[s, n_rope % 2, :], t2[s, :], ALU.add)
                        else:
                            last = V.tensor_tensor(kT[:, i, NP_TOK:TOK], t1[:, n_rope % 2, :], t2, ALU.add)
                        last.then_inc(rope_done, 1)
                        n_rope += 1
                for i in range(HALF + 2):
                    h = HALF * g + i
                    if i < HALF:
                        for r in range(TT):
                            n = TT * h + r
                            w = P if r == 0 else TOK
                            for c in range(2):
                                filled(dve, ("S", h, r, c))
                                V.tensor_reduce(out=nm[:, n % 6, c:c + 1], in_=bank(("S", h, r, c))[:, 0:w], axis=AX.X, op=ALU.max,
                                                negate=True).then_inc(max_ready, 1)
                        for r in range(TT):
                            n = TT * h + r
                            w = P if r == 0 else TOK
                            emptied(dve, ("S", h, r, 1))
                            link(V.reciprocal(rc[:, 0:2], sm[:, n % 6, :]))
                            link(V.tensor_tensor(rc[:, 2:3], rc[:, 1:2], lam_s[:, 0:1], ALU.mult))
                            if h:
                                filled(dve, ("aT", h - 1, r))
                            link(V.tensor_scalar(aw[:, r, 0:w], pr[:, n % 2, 0, 0:w], rc[:, 0:1], None, ALU.mult))
                            V.scalar_tensor_tensor(out=aw[:, r, 0:w], in0=pr[:, n % 2, 1, 0:w], scalar=rc[:, 2:3],
                                                   in1=aw[:, r, 0:w], op0=ALU.mult, op1=ALU.add).then_inc(a_ready, 1)
                    if 1 <= i <= HALF:
                        filled(dve, ("o", h - 1))
                        V.tensor_copy(oT[:, h - 1, :], bank(("o", h - 1))[:, 0:TOK]).then_inc(evac["dve"], 1)
                    if i >= 2:
                        filled(dve, ("oss", h - 2))
                        if i == 2:
                            dve.wait_ge(stored_k, 16 * (g + 1))
                        V.tensor_copy(ss[:, i - 2, :], bank(("oss", h - 2))[:, 0:TOK]).then_inc(evac["dve"], 1)
                dve.wait_ge(ssq_root, g + 1)
                link(V.reciprocal(ss[:, :, :], ss[:, :, :]))
                V.scalar_tensor_tensor(out=oT[:, HALF * g:HALF * g + HALF, :], in0=oT[:, HALF * g:HALF * g + HALF, :],
                                       scalar=subg[:, :], in1=ss[:, :, :], op0=ALU.mult, op1=ALU.mult).then_inc(oT_ready, 1)
            ada(0, range(4, 12))
            ada(1, range(12))
            dve.wait_ge(mod_ready, 24)
            for ft in range(KT):
                residual(("wo", ft), ft, 0, 2)

            def experts(l):
                m = M[l]
                norm(2 * l + 1)
                filled(dve, ("logit", l))
                V.tensor_copy(wm["lg"][0:NE, :], bank(("logit", l))[0:NE, 0:TOK]).then_inc(evac["dve"], 1)
                for i in range(0, 2 * TT, 2):
                    filled(dve, ("htok", l, i))
                    V.tensor_copy(htok[:, i // 2, 0:512], bank(("htok", l, i))).then_inc(evac["dve"], 1)
                s3 = v3("s", TT)
                selb = v3("selb", TT)
                b3 = rbias[:, :].unsqueeze(1).broadcast_to([P, TT, NE])
                emptied(dve, ("logitT", l))
                link(V.tensor_tensor(selb, s3, b3, ALU.add))
                g4 = wm["selb"].rearrange("p (g e) -> p g e", e=EPG)
                pair = wm["pair"].rearrange("p (g n) -> p g n", n=6)
                V.tensor_tensor(pair[:, :, 0:3], g4[:, :, 0:3], g4[:, :, 1:4], ALU.add)
                V.tensor_tensor(pair[:, :, 3:5], g4[:, :, 0:2], g4[:, :, 2:4], ALU.add)
                link(V.tensor_tensor(pair[:, :, 5:6], g4[:, :, 0:1], g4[:, :, 3:4], ALU.add))
                link(V.tensor_reduce(out=wm["gs"], in_=pair, axis=AX.X, op=ALU.max))
                gs3, gw3 = v3("gs", TT), v3("gw", TT)

                def first_largest(out3, in3, mx, w3, wx, order, n):
                    link(V.tensor_reduce(out=mx, in_=in3, axis=AX.X, op=ALU.max))
                    link(V.tensor_tensor(w3, in3, mx.unsqueeze(2).broadcast_to([P, TT, n]), ALU.is_ge))
                    link(V.tensor_tensor(w3, w3, order.unsqueeze(1).broadcast_to([P, TT, n]), ALU.mult))
                    link(V.tensor_reduce(out=wx, in_=w3, axis=AX.X, op=ALU.max))
                    link(V.tensor_tensor(out3, w3, wx.unsqueeze(2).broadcast_to([P, TT, n]), ALU.is_equal))

                first_largest(v3("ing", TT), gs3, wm["gm"], gw3, wm["gx"], table(base_sb, base_at, "first4"), NG)
                link(V.tensor_scalar(wm["pen"], wm["ing"], BIG, -BIG, ALU.mult, ALU.add))
                bcast4 = lambda name: wm[name].unsqueeze(2).broadcast_to([P, TT * NG, EPG])
                link(V.tensor_tensor(g4, g4, bcast4("ing"), ALU.mult))
                link(V.tensor_tensor(g4, g4, bcast4("pen"), ALU.add))
                mm_ = wm["m"].rearrange("p (c t e) -> p c t e", c=2, t=TT)
                wt = v3("wt", 2)
                for c in range(2):
                    first_largest(mm_[:, c], selb, wm["mx"], v3("w", TT), wm["wx"], table(base_sb, base_at, "first16"), NE)
                    if c == 0:
                        link(V.scalar_tensor_tensor(out=wm["selb"], in0=wm["m"][:, 0:TT * NE], scalar=-2 * BIG, in1=wm["selb"],
                                                    op0=ALU.mult, op1=ALU.add))
                link(V.tensor_tensor(wm["M"], wm["m"][:, 0:TT * NE], wm["m"][:, TT * NE:], ALU.add))
                V.sem_inc(m["chosen"], 1)
                for c in range(2):
                    link(V.tensor_tensor(v3("pick", TT), mm_[:, c], s3, ALU.mult))
                    link(V.tensor_reduce(out=wt[:, c], in_=v3("pick", TT), axis=AX.X, op=ALU.add))
                link(V.tensor_tensor(wm["den"], wt[:, 0], wt[:, 1], ALU.add))
                link(V.reciprocal(wm["den"], wm["den"]))
                link(V.tensor_tensor(wt, wt, wm["den"].unsqueeze(1).broadcast_to([P, 2, TT]), ALU.mult))
                filled(dve, ("rank", l))
                V.tensor_copy(wm["rk"], bank(("rank", l))[:, 0:(TT + 1) * NE]).then_inc(evac["dve"], 1)
                emptied(dve, ("rank", l))
                rank, count = v3("rk", TT + 1)[:, 0:TT], wm["rk"][:, TT * NE:]
                link(V.tensor_scalar(wm["nov"], count, float(BLK), None, ALU.is_gt))
                for n in range(2, TOK // BLK):
                    link(V.scalar_tensor_tensor(out=wm["nov"], in0=count, scalar=float(BLK * n), in1=wm["nov"],
                                                op0=ALU.is_gt, op1=ALU.add))
                V.memset(wm["cum"][:, 0:1], 0.0)
                link(V.tensor_tensor_scan(wm["cum"][:, 1:NE + 1], ones[:, 0:NE], wm["nov"], 0.0, ALU.mult, ALU.add))
                V.tensor_copy(RT[l][0:1, :], wm["cum"][0:1, :])
                R3, M3, hi = v3("R", TT), v3("M", TT), v3("hi", TT)
                V.memset(R3[:, :, NE:NE + 2], -1.0)
                link(V.scalar_tensor_tensor(out=R3[:, :, 0:NE], in0=rank, scalar=1.0, in1=M3, op0=ALU.add, op1=ALU.mult))
                link(V.tensor_scalar(R3[:, :, 0:NE], R3[:, :, 0:NE], -1.0, None, ALU.add))
                V.sem_inc(m["routed"], 1)
                row0 = table(base_sb, base_at, "row0")
                link(V.scalar_tensor_tensor(out=wm["dd"], in0=wm["cum"][:, 0:NE], scalar=float(BLK), in1=row0, op0=ALU.mult, op1=ALU.subtract))
                link(V.tensor_scalar(wm["dd"], wm["dd"], float((NE - 1) * BLK), None, ALU.add))
                link(V.tensor_scalar(hi, rank, float(BLK), None, ALU.is_ge))
                link(V.tensor_tensor(hi, hi, wm["dd"].unsqueeze(1).broadcast_to([P, TT, NE]), ALU.mult))
                link(V.tensor_tensor(hi, hi, rank, ALU.add))
                link(V.tensor_tensor(hi, hi, row0.unsqueeze(1).broadcast_to([P, TT, NE]), ALU.add))
                row = v3("row", 2)
                for c in range(2):
                    link(V.tensor_tensor(v3("pick", TT), mm_[:, c], hi, ALU.mult))
                    link(V.tensor_reduce(out=row[:, c], in_=v3("pick", TT), axis=AX.X, op=ALU.add))
                V.tensor_copy(wm["idx"].bitcast(I32), wm["row"]).then_inc(m["idx"], 1)

                dve.sem_inc(m["gated"], 2)
                dve.sem_inc(m["y_dve"], 1)

                def select(pair):
                    V.tensor_tensor(sel, iota[:, 0:BLK].unsqueeze(1).unsqueeze(1).broadcast_to([P, TT, 2, BLK]),
                                    R3[:, :, ds(pair * 2, 2)].unsqueeze(3).broadcast_to([P, TT, 2, BLK]),
                                    ALU.is_equal).then_inc(m["sel"], 1)

                def take_xs(pair, par):
                    dve.wait_ge(m["gathered"], pair + 1)
                    V.tensor_copy(xs[:, par, 4:8, :].rearrange("p k s -> p (k s)"), psum[:, 3, :]).then_inc(m["xs_dve"], 1)

                def overflow(e):
                    lo = dve.value_load(RT[l][0:1, ds(e, 1)], min_val=0, max_val=MAXOV)
                    hi_ = dve.value_load(RT[l][0:1, ds(e + 1, 1)], min_val=0, max_val=MAXOV)
                    ov = psum[:, 7, :]
                    with dve.If(lo < hi_):
                        with dve.Fori(lo, hi_) as o:
                            V.tensor_scalar(R3[:, :, ds(e, 1)], R3[:, :, ds(e, 1)], -float(BLK), None, ALU.add).then_inc(m["o_ranks"], 1)
                            dve.wait_ge(m["o_ranks"], o + 1)
                            V.tensor_tensor(osel, iota[:, 0:BLK].unsqueeze(1).broadcast_to([P, TT, BLK]),
                                            R3[:, :, ds(e, 1)].broadcast_to([P, TT, BLK]), ALU.is_equal).then_inc(m["o_sel"], 1)
                            dve.wait_ge(m["o_gathered"], o + 1)
                            V.tensor_copy(wm["ox"], ov).then_inc(m["o_xs"], 1)
                            dve.wait_ge(m["o_silu"], o + 1)
                            V.tensor_tensor(oa[0:BLK, :], osg[BLK:P, :], ov[BLK:P, :], ALU.mult).then_inc(m["o_gated"], 1)
                            dve.wait_ge(m["o_T"], o + 1)
                            V.tensor_copy(wm["oaT"], ov[:, 0:256]).then_inc(m["o_aT"], 1)
                            dve.wait_ge(m["o_down"], o + 2)
                            dve.wait_ge(m["o_stored"], o * 32 + 32)
                            V.tensor_copy(oy, ov).then_inc(m["o_y"], 1)

                select(0)
                take_xs(0, 0)
                with dve.Fori(0, NE // 4) as it:
                    for par in range(2):
                        q = it * 2 + par
                        dve.wait_ge(m["gathered"], q + 1)
                        select(q + 1)
                        for x in range(2):
                            e = q * 2 + x
                            dve.wait_ge(m["silu"], e + 1)
                            V.tensor_tensor(ea[0:BLK, x, :], sg[BLK:P, x, :], psum[BLK:P, x, :], ALU.mult).then_inc(m["gated"], 1)
                            overflow(e)
                        take_xs(q + 1, 1 - par)
                        dve.wait_ge(m["T"], q * 2 + 2)
                        V.tensor_copy(eaT[:, 1].rearrange("p k s -> p (k s)"), psum[:, 1, 0:256]).then_inc(m["aT_dve"], 1)
                        dve.wait_ge(m["down"], q * 2 + 2)
                        dve.wait_ge(m["stored1"], q * 32 + 32)
                        V.tensor_copy(ysb[:, 1, :], psum[:, 6, :]).then_inc(m["y_dve"], 1)
                for t in range(TT):
                    dve.wait_ge(m["picked"], 32 * TT)
                    link(V.tensor_scalar(ytok[:, t, :], yg[0][:, t, :], wt[:, 0, t:t + 1], None, ALU.mult))
                    V.scalar_tensor_tensor(out=ytok[:, t, :], in0=yg[1][:, t, :], scalar=wt[:, 1, t:t + 1], in1=ytok[:, t, :],
                                           op0=ALU.mult, op1=ALU.add).then_inc(m["ytok"], 1)
                for ft in range(KT):
                    residual(("y", l, ft), ft, l, 5)

            experts(0)

            norm(2)
            dve.wait_ge(in_ret, 32)
            rcos, rsin = table(ret_tab, ret_at, "cos"), table(ret_tab, ret_at, "sin")
            keep = [table(dist_tab, dist_at, f"keep_{s}") for s in "fb"]
            I = lambda ap: ap.bitcast(I32)
            for h in range(RH):
                for j, (kind, t_) in enumerate((("rq", rq), ("rk", rk))):
                    emptied(dve, (kind, h, 1))
                    if 2 * h + j:
                        dve.wait_ge(rope_ret, 2 * h + j)
                    x1, x2 = t_[:, 0, P:TOK], t_[:, 1, P:TOK]
                    c2 = rcos.unsqueeze(1).broadcast_to([P, 2, NS_TOK])
                    V.tensor_tensor(rtmp[:, 0], t_[:, :, P:TOK], c2, ALU.mult)
                    V.tensor_tensor(rtmp[:, 1, 0], x2, rsin, ALU.mult)
                    link(V.tensor_tensor(rtmp[:, 1, 1], x1, rsin, ALU.mult))
                    V.tensor_tensor(x1, rtmp[:, 0, 0], rtmp[:, 1, 0], ALU.subtract)
                    V.tensor_tensor(x2, rtmp[:, 0, 1], rtmp[:, 1, 1], ALU.add).then_inc(rope_ret, 1)
                dve.wait_ge(rope_ret, 2 * h + 2)
                dve.wait_ge(decay_ready, 4 * h + 4)
                for d in range(2):
                    V.tensor_tensor(qd[:, d], rq[:, :, P:TOK], qe[:, d, :].unsqueeze(1).broadcast_to([P, 2, NS_TOK]), ALU.mult).then_inc(qd_ready, 1)
                for d in range(2):
                    link(V.tensor_tensor(rE[:, d, 0:NS_TOK + 1], rE[:, d, 0:NS_TOK + 1], keep[d], ALU.mult))
                for t in range(TT):
                    filled(dve, ("rv", h, t))
                    V.tensor_copy(rv[:, t, :], bank(("rv", h, t))).then_inc(evac["dve"], 1)
                if h:
                    filled(dve, ("rs", h - 1, 1, 1))
                filled(dve, ("rkT", h))
                V.tensor_scalar(kd[:, 0, :], bank(("rkT", h))[:, 0:RDK], rE[:, 0, NS_TOK:NS_TOK + 1], None, ALU.mult)
                V.tensor_scalar(kd[:, 1, :], bank(("rkT", h))[:, 0:RDK], rE[:, 1, NS_TOK:NS_TOK + 1], None, ALU.mult).then_inc(evac["dve"], 1)
                filled(dve, ("rA", h, 0))
                b = bank(("rA", h, 0))
                V.tensor_tensor(rA[:, 0, 0:P], b[:, 0:P], rE[:, 0, 0:P], ALU.mult)
                V.tensor_tensor(rA[:, 0, P:TOK], b[:, P:TOK], rE[:, 0, 0:NS_TOK], ALU.mult)
                V.tensor_tensor(rA[:, 1, 0:2 * P].rearrange("p (a t) -> p a t", a=2), b[:, 0:2 * P].rearrange("p (a t) -> p a t", a=2),
                                rE[:, 1, P:NS_TOK].unsqueeze(1).broadcast_to([P, 2, P]), ALU.mult).then_inc(evac["dve"], 1)
                filled(dve, ("rA", h, 1))
                b = bank(("rA", h, 1))
                V.tensor_tensor(rA[:, 0, TOK:TOK + P], b[:, P:NS_TOK], rE[:, 0, 0:P], ALU.mult)
                V.tensor_tensor(rA[:, 1, 2 * P:4 * P], b[:, 0:NS_TOK], rE[:, 1, 0:NS_TOK], ALU.mult).then_inc(evac["dve"], 1)
                for t in range(TT):
                    n = TT * h + t
                    for d in range(2):
                        filled(dve, ("ro", h, t, d))
                        link(V.bn_stats(out=bst[:, d, :], in_=bank(("ro", h, t, d))))
                        link(V.bn_aggr(out=mv[:, d, :], in_=bst[:, d, :]))
                    if n:
                        emptied(dve, ("ro",) + (divmod(n - 1, TT)[0], divmod(n - 1, TT)[1], 1))
                    var, y, u = nw[:, 0:2], nw[:, 2:4], nw[:, 4:6]
                    link(V.tensor_scalar(var, mv[:, :, 1], EPS, None, ALU.add))
                    link(V.tensor_scalar(I(u), I(var), 1, None, ALU.logical_shift_right))
                    link(V.tensor_scalar(I(y), I(u), -1.0, float(0x5F3759DF), ALU.mult, ALU.add))
                    for _ in range(4):
                        link(V.tensor_tensor(u, y, y, ALU.mult))
                        link(V.tensor_tensor(u, u, var, ALU.mult))
                        link(V.tensor_scalar(u, u, -0.5, 1.5, ALU.mult, ALU.add))
                        link(V.tensor_tensor(y, y, u, ALU.mult))
                    link(V.tensor_tensor(u, mv[:, :, 0], y, ALU.mult))
                    V.tensor_scalar(nw[:, 12:14], u, -1.0, None, ALU.mult).then_inc(stat_ready, 1)
                    emptied(dve, ("ro", h, t, 1))
                    V.tensor_tensor(rn[:, 1, :], rn[:, 1, :], rg[:, 1, t, :], ALU.mult).then_inc(n_ready, 1)
                    dve.wait_ge(n_ready, n + 1)
                    dve.wait_ge(gate_pool, n + 1)
                    if h:
                        filled(dve, ("roT", h - 1, t))
                    V.tensor_tensor(ro[:, t, :], rn[:, 0, :], rn[:, 1, :], ALU.add).then_inc(ro_ready, 1)
            for ft in range(KT):
                residual(("rwo", ft), ft, 1, 2)
            experts(1)
            norm(4)
            for i in range(0, 2 * TT, 2):
                filled(dve, ("yout", i))
                V.tensor_copy(yo(i), bank(("yout", i))).then_inc(evac["dve"], 1)

        @block.gpsimd
        def _(pool):
            G = nc.gpsimd
            G.memset(zrow, 0.0).then_inc(zero_ready, 1)
            G.memset(ones[:, :], 1.0).then_inc(pool_init, 1)
            G.memset(cond[:, :, :], 0.0).then_inc(pool_init, 1)
            pool.wait_ge(pool_init, 2)
            n_bc = 0
            for n, name in enumerate(("da_lambda_q1", "da_lambda_k1", "da_lambda_q2", "da_lambda_k2")):
                pool.dma_start(lamrow[:, n, :], ins[name].broadcast_to([P, HD])).then_inc(in_bc, 16)
            pool.dma_start(dec[:, 0, 0:RH], ins["ret_decay_fwd"].broadcast_to([P, RH])).then_inc(in_bc, 16)
            pool.dma_start(dec[:, 0, RH:2 * RH], ins["ret_decay_bwd"].broadcast_to([P, RH])).then_inc(in_bc, 16)
            pool.dma_start(rbias[:, :], ins["router_bias"].unsqueeze(0).broadcast_to([P, NE])).then_inc(in_bc, 16)
            pool.dma_start(wr[:, :, :], ins["w_router"].rearrange("(k p) e -> p k e", p=P)).then_inc(in_bc, 16)
            pool.wait_ge(in_x, 32)
            emptied(pool, ("x", KT - 1))
            G.memset(qz[64:P, 0], 0.0).then_inc(pool_init, 1)
            pool.wait_ge(pool_init, 3)
            G.memset(qz[0:64, 1], 0.0).then_inc(pool_init, 1)
            pool.wait_ge(pool_init, 4)
            cos = table(att_tab, att_at, "cos")
            pool.wait_ge(in_ck, 48)
            n_rope = 0
            for g in range(2):
                for kind in "qk":
                    for i in range(HALF):
                        h = HALF * g + i
                        emptied(pool, (kind, h))
                        r = raw[:, n_rope % 2, :]
                        if kind == "k":
                            G.tensor_copy(kT[:, i, 0:NP_TOK], r[:, 0:NP_TOK])
                        if n_rope >= 2:
                            pool.wait_ge(rope_done, n_rope - 1)
                        G.tensor_tensor(t1[:, n_rope % 2, :], r[:, NP_TOK:TOK], cos, ALU.mult).then_inc(rope_pool, 1)
                        n_rope += 1

            def pick_rows(l):
                m = M[l]
                pool.wait_ge(m["routed"], 1)
                total = pool.value_load(RT[l][0:1, NE:NE + 1], min_val=0, max_val=MAXOV)
                pool.wait_ge(m["idx"], 1)
                pool.wait_ge(m["stored0"], 32 * (NE // 2 + 1))
                pool.wait_ge(m["stored1"], 32 * (NE // 2 + 1))
                pool.wait_ge(m["o_stored"], total * 32 + 32)
                settle(pool, l)
                idx = wm["idx"].bitcast(mybir.dt.uint32).rearrange("p (c t) -> p c t", c=2)
                for t in range(TT):
                    for c in range(2):
                        pool.indirect_dma_start(out=yg[c][:, t, :], out_offset=None, in_=scratch,
                                                in_offset=bass.IndirectOffsetOnAxis(ap=idx[:, c, t:t + 1], axis=0)).then_inc(m["picked"], 16)

            pool.sem_inc(M[0]["o_down"], 1)
            pool.sem_inc(M[1]["o_down"], 1)
            pick_rows(0)
            for h in range(RH):
                for t in range(TT):
                    emptied(pool, ("ro", h, t, 0))
                    G.tensor_tensor(rn[:, 0, :], rn[:, 0, :], rg[:, 0, t, :], ALU.mult).then_inc(gate_pool, 1)
            pick_rows(1)


INPUTS = ["x_prompt", "x_sample", "cache_attn_k", "cache_attn_v", "state_ret_fwd", "state_ret_bwd", "c", "c_ctx", "w_ada",
          "b_ada", "norm_mix_g", "norm_ffn_g", "final_norm_g", "da_w_qkv", "da_lambda_q1", "da_lambda_k1", "da_lambda_q2",
          "da_lambda_k2", "da_subln_g", "da_w_o", "ret_w_qkv", "ret_w_gate_fwd", "ret_w_gate_bwd", "ret_decay_fwd",
          "ret_decay_bwd", "ret_w_o", "w_router", "router_bias", "moe_w_gate", "moe_w_up", "moe_w_down"]
OUTPUTS = [("y_prompt", (1, NP_TOK, D)), ("y_sample", (1, NS_TOK, D)), ("new_attn_k", (1, 1, NP_TOK, HEADS, 2, HD)),
           ("new_attn_v", (1, 1, NP_TOK, HEADS, HV)), ("new_ret_fwd", (1, 1, RH, RDK, RDV)), ("new_ret_bwd", (1, 1, RH, RDK, RDV))]


def kernel(**inputs):
    import concourse.bacc as bacc
    from concourse.bass_utils import run_bass_kernel_spmd

    nc = bacc.Bacc("TRN2", target_bir_lowering=False, num_devices=1)
    arrays, ins = {}, {}
    for name in INPUTS:
        a = np.ascontiguousarray(inputs[name])
        arrays[f"in_{name}"] = a
        ins[name] = nc.dram_tensor(f"in_{name}", a.shape, mybir.dt.from_np(a.dtype), kind="ExternalInput").ap()
    outs = [nc.dram_tensor(f"out_{name}", shape, mybir.dt.float32, kind="ExternalOutput").ap() for name, shape in OUTPUTS]
    scratch = nc.dram_tensor("expert_rows", ((NE + MAXOV) * BLK, D), mybir.dt.float32, kind="Internal").ap()
    trunk_kernel(nc, ins, outs, scratch)
    r = run_bass_kernel_spmd(nc, [arrays], core_ids=[0])
    return tuple(r.results[0][f"out_{name}"] for name, _ in OUTPUTS)
```
